# Optimizing a Trainium2 kernel written in Bass

```python
import math
import jax, jax.numpy as jnp
from jax import lax
import numpy as np

D_MODEL = 1024
BATCH = 1
SEQ = 512
DEPTH = 2

EPS = 1e-6
N_EVEN = (DEPTH + 1) // 2
N_ODD = DEPTH // 2
A_WIDTH = D_MODEL // 2
A_GROUPS = 8
CONV_A_WIDTH = 31
B_WIDTH = D_MODEL // 2
B_HEADS = 4
B_HEAD_DIM = B_WIDTH // B_HEADS
CHUNK = 128
EVEN_IN = 2 * A_WIDTH + 2 * B_WIDTH
EVEN_MIX = A_WIDTH + B_WIDTH
C_WIDTH = D_MODEL
CONV_C_WIDTH = 3
ODD_IN = 3 * C_WIDTH
PEER_HEADS = 8
N_KEYS = 128
N_EXPERTS = N_KEYS * N_KEYS
D_KEY = 256
D_KEY_HALF = D_KEY // 2
PEER_TOPK = 16
PEER_CHUNK = 128

kernel_name = "hybrid_conv_gmlp_shortconv_peer_adaln"

def rms_norm(x, g):
    xf = x.astype(jnp.float32)
    y = xf * lax.rsqrt(jnp.mean(xf * xf, axis=-1, keepdims=True) + EPS)
    return (y * g.astype(jnp.float32)).astype(x.dtype)

def layer_norm(x, g, b):
    xf = x.astype(jnp.float32)
    mu = jnp.mean(xf, axis=-1, keepdims=True)
    var = jnp.mean(jnp.square(xf - mu), axis=-1, keepdims=True)
    y = (xf - mu) * lax.rsqrt(var + EPS)
    return (y * g.astype(jnp.float32) + b.astype(jnp.float32)).astype(x.dtype)

def causal_dwconv(x, w):
    k, ch = w.shape
    return lax.conv_general_dilated(
        x, w.astype(x.dtype)[:, None, :], window_strides=(1,), padding=[(k - 1, 0)],
        dimension_numbers=("NWC", "WIO", "NWC"), feature_group_count=ch)

def modulate(h, shift, scale):
    return h * (1.0 + scale[:, None, :]) + shift[:, None, :]

def conv_gmlp_mixer(h, w_in, conv_w, conv_b, cln_g, cln_b, gln_g, gln_b, ws, bs, w_out):
    bsz, seq, _ = h.shape
    z = h @ w_in.astype(h.dtype)
    za, zb = z[..., :2 * A_WIDTH], z[..., 2 * A_WIDTH:]
    a = za[..., :A_WIDTH] * jax.nn.sigmoid(za[..., A_WIDTH:])
    a = causal_dwconv(a, conv_w) + conv_b.astype(h.dtype)
    a = jax.nn.silu(layer_norm(a, cln_g, cln_b))
    zb = jax.nn.gelu(zb, approximate=False)
    u, v = zb[..., :B_WIDTH], zb[..., B_WIDTH:]
    v = layer_norm(v, gln_g, gln_b)
    v = v.reshape(bsz, seq // CHUNK, CHUNK, B_HEADS, B_HEAD_DIM)
    causal = jnp.tril(jnp.ones((CHUNK, CHUNK), dtype=bool))
    ws_m = jnp.where(causal[None], ws, 0.0).astype(h.dtype)
    mixed = jnp.einsum("hts,bnshc->bnthc", ws_m, v) + bs.T.astype(h.dtype)[None, None, :, :, None]
    bout = u * mixed.reshape(bsz, seq, B_WIDTH)
    return jnp.concatenate([a, bout], axis=-1) @ w_out.astype(h.dtype)

def short_conv_mixer(h, w_in, conv_w, w_out):
    z = h @ w_in.astype(h.dtype)
    gb, gc, xin = z[..., :C_WIDTH], z[..., C_WIDTH:2 * C_WIDTH], z[..., 2 * C_WIDTH:]
    y = gb * causal_dwconv(gc * xin, conv_w)
    return y @ w_out.astype(h.dtype)

def peer(h, wq, subkeys, u_tab, v_tab):
    bsz, seq, d = h.shape
    sk = subkeys.astype(jnp.float32)

    def chunk_fn(hc):
        t = hc.shape[0]
        q = (hc @ wq.astype(hc.dtype)).reshape(t, PEER_HEADS, 2, D_KEY_HALF).astype(jnp.float32)
        s = jnp.einsum("thpk,pnk->thpn", q, sk)
        s1, i1 = lax.top_k(s[:, :, 0], PEER_TOPK)
        s2, i2 = lax.top_k(s[:, :, 1], PEER_TOPK)
        cand = (s1[..., :, None] + s2[..., None, :]).reshape(t, PEER_HEADS, PEER_TOPK * PEER_TOPK)
        best, j = lax.top_k(cand, PEER_TOPK)
        e = (jnp.take_along_axis(i1, j // PEER_TOPK, axis=-1) * N_KEYS
             + jnp.take_along_axis(i2, j % PEER_TOPK, axis=-1))
        gate = jax.nn.softmax(best, axis=-1)
        ue = u_tab[e].astype(hc.dtype)
        act = jax.nn.gelu(jnp.einsum("thkd,td->thk", ue, hc).astype(jnp.float32), approximate=False)
        ve = v_tab[e].astype(hc.dtype)
        return jnp.einsum("thk,thkd->td", (gate * act).astype(hc.dtype), ve)

    out = lax.map(chunk_fn, h.reshape(-1, PEER_CHUNK, d))
    return out.reshape(bsz, seq, d)

def setup_inputs(seed: int = 0) -> dict:
    key = jax.random.key(seed)
    ks = jax.random.split(key, 32)
    f32 = jnp.float32
    nrm = lambda k, shape, s: jax.random.normal(k, shape, f32) * s
    D = D_MODEL
    return {
        "x": nrm(ks[0], (BATCH, SEQ, D), 1.0),
        "c": nrm(ks[1], (BATCH, D), 1.0),
        "mod_w": nrm(ks[2], (DEPTH, D, 6 * D), 0.5 * D ** -0.5),
        "mod_b": nrm(ks[3], (DEPTH, 6 * D), 0.02),
        "norm1_g": 1.0 + nrm(ks[4], (DEPTH, D), 0.02),
        "norm2_g": 1.0 + nrm(ks[5], (DEPTH, D), 0.02),
        "ev_w_in": nrm(ks[6], (N_EVEN, D, EVEN_IN), D ** -0.5),
        "ev_conv_w": nrm(ks[7], (N_EVEN, CONV_A_WIDTH, A_WIDTH), CONV_A_WIDTH ** -0.5),
        "ev_conv_b": nrm(ks[8], (N_EVEN, A_WIDTH), 0.02),
        "ev_cln_g": 1.0 + nrm(ks[9], (N_EVEN, A_WIDTH), 0.02),
        "ev_cln_b": nrm(ks[10], (N_EVEN, A_WIDTH), 0.02),
        "ev_gln_g": 1.0 + nrm(ks[11], (N_EVEN, B_WIDTH), 0.02),
        "ev_gln_b": nrm(ks[12], (N_EVEN, B_WIDTH), 0.02),
        "ev_ws": nrm(ks[13], (N_EVEN, B_HEADS, CHUNK, CHUNK), CHUNK ** -0.5),
        "ev_bs": nrm(ks[14], (N_EVEN, B_HEADS, CHUNK), 0.02),
        "ev_w_out": nrm(ks[15], (N_EVEN, EVEN_MIX, D), EVEN_MIX ** -0.5),
        "od_w_in": nrm(ks[16], (N_ODD, D, ODD_IN), D ** -0.5),
        "od_conv_w": nrm(ks[17], (N_ODD, CONV_C_WIDTH, C_WIDTH), CONV_C_WIDTH ** -0.5),
        "od_w_out": nrm(ks[18], (N_ODD, C_WIDTH, D), C_WIDTH ** -0.5),
        "pk_wq": nrm(ks[19], (DEPTH, D, PEER_HEADS * D_KEY), D ** -0.5),
        "pk_subkeys": nrm(ks[20], (DEPTH, 2, N_KEYS, D_KEY_HALF), D_KEY_HALF ** -0.5),
        "pk_u": nrm(ks[21], (DEPTH, N_EXPERTS, D), D ** -0.5),
        "pk_v": nrm(ks[22], (DEPTH, N_EXPERTS, D), 1.0),
        "final_g": 1.0 + nrm(ks[23], (D,), 0.02),
    }

def reference(x, c, mod_w, mod_b, norm1_g, norm2_g, ev_w_in, ev_conv_w, ev_conv_b, ev_cln_g,
              ev_cln_b, ev_gln_g, ev_gln_b, ev_ws, ev_bs, ev_w_out, od_w_in, od_conv_w, od_w_out,
              pk_wq, pk_subkeys, pk_u, pk_v, final_g):
    c_act = jax.nn.silu(c)
    for l in range(DEPTH):
        mod = c_act @ mod_w[l].astype(c.dtype) + mod_b[l].astype(c.dtype)
        sh1, sc1, g1, sh2, sc2, g2 = jnp.split(mod.astype(x.dtype), 6, axis=-1)
        h = modulate(rms_norm(x, norm1_g[l]), sh1, sc1)
        i = l // 2
        if l % 2 == 0:
            y = conv_gmlp_mixer(h, ev_w_in[i], ev_conv_w[i], ev_conv_b[i], ev_cln_g[i], ev_cln_b[i],
                                ev_gln_g[i], ev_gln_b[i], ev_ws[i], ev_bs[i], ev_w_out[i])
        else:
            y = short_conv_mixer(h, od_w_in[i], od_conv_w[i], od_w_out[i])
        x = x + g1[:, None, :] * y
        h = modulate(rms_norm(x, norm2_g[l]), sh2, sc2)
        x = x + g2[:, None, :] * peer(h, pk_wq[l], pk_subkeys[l], pk_u[l], pk_v[l])
    return rms_norm(x, final_g)


_drawn_inputs = setup_inputs


def setup_inputs(seed=0):
    import zlib

    import numpy as np

    out = dict(_drawn_inputs(seed))
    spreads = {}
    factors = {'ev_cln_g': 3.003,
     'ev_cln_b': 3.17,
     'ev_gln_g': 3.475,
     'ev_gln_b': 3.734,
     'ev_bs': 3.338,
     'final_g': 2.901}
    for name, (base, spread) in spreads.items():
        noise = np.random.default_rng([zlib.crc32(name.encode()), seed]).standard_normal(out[name].shape)
        drawn = base * np.exp(spread * noise) if base else spread * noise
        out[name] = __import__('jax').numpy.asarray(drawn.astype(out[name].dtype))
    for name, factor in factors.items():
        out[name] = (out[name] * factor).astype(out[name].dtype)
    return out
```

```python
from contextlib import ExitStack

import numpy as np

import concourse.bass as bass
from concourse import mybir

F32 = mybir.dt.float32
F32R = mybir.dt.float32r
BF16 = mybir.dt.bfloat16
U32 = mybir.dt.uint32
I32 = mybir.dt.int32
ALU = mybir.AluOpType
ACT = mybir.ActivationFunctionType
AX_X = mybir.AxisListType.X

P = 128
D = 1024
KC = D // P
T = 512
EPS = 1e-6
AC = 512 // P
TAPS = 31
HEADS = 8
TOPK = 16
NK = 128
TB = T // P
LOWEST = -3.0e38

MOD_TILES = 2 * 6 * KC
EV_IN, EV_OUT, OD_IN, OD_OUT = 16, KC, 3 * KC, KC
Q_TILES, EXPERT_TILES = 2 * HEADS, NK
BASE = {}
EVAC = {}
_g = _b = 0
for _name, _n, _banked in [("ev_in", EV_IN, 1), ("ev_out", EV_OUT, 1), ("q0", Q_TILES, 1), ("u0", EXPERT_TILES, 1),
                           ("v0", EXPERT_TILES, 0), ("od_in", OD_IN, 1), ("od_out", OD_OUT, 1), ("q1", Q_TILES, 1),
                           ("u1", EXPERT_TILES, 1), ("v1", EXPERT_TILES, 0)]:
    BASE[_name], EVAC[_name] = _g, _b
    _g += _n
    _b += _n * _banked
TILES = _g
RING = 4
assert all(b % RING == 0 for b in BASE.values()) and MOD_TILES % RING == 0

TILES_PER_BLOCK = 12
GROUP = 8
HALF = 64
TAIL_TILES = EXPERT_TILES - TB * TILES_PER_BLOCK - T // GROUP

ROWS = [(a, TOPK // (a + 1)) for a in range(TOPK // 2)]
OFFS = np.cumsum([0] + [n for _, n in ROWS]).tolist()
NCAND = OFFS[-1] + TOPK // 2

COLS = {}
_c = 0
for _name, _n in [("c", KC), ("mod_b", MOD_TILES), ("norm1_g", 2 * KC), ("norm2_g", 2 * KC), ("conv_w", AC * TAPS),
                  ("conv_b", AC), ("cln_g", AC), ("cln_b", AC), ("gln_g", AC), ("gln_b", AC),
                  ("od_conv_w", 3 * KC), ("final_g", KC)]:
    COLS[_name] = _c
    _c += _n
NCOLS = _c


def build(nc, stream, mod_stream, x_in, cols_in, sk_in, ws_in, bs_in, out, act_dram, gate_dram):
    with ExitStack() as ctx:
        def sb(name, shape, dt=F32):
            return ctx.enter_context(nc.sbuf_tensor(name, shape, dt))

        def sem(name):
            return ctx.enter_context(nc.semaphore(name))

        ps = [ctx.enter_context(nc.psum_tensor(f"bank{i}", [P, 512], F32)) for i in range(8)]

        x = sb("x", [P, KC, T])
        h_hi = sb("h_hi", [P, KC, T], F32R)
        h_lo = sb("h_lo", [P, KC, T], F32R)
        w_raw = sb("w_raw", [P, RING, D])
        w_hi = sb("w_hi", [P, 2, D], F32R)
        w_lo = sb("w_lo", [P, 2, D], F32R)
        shared = sb("shared", [P, 16384])
        oh_i = sb("oh_i", [P, 2, GROUP, NK], BF16)
        oh_j = sb("oh_j", [P, 2, GROUP, 3, NK], BF16)
        act_ring = sb("act_ring", [P, RING, T])
        i_t = sb("i_t", [P, T])
        j_t = sb("j_t", [P, T])
        gate_t = sb("gate_t", [P, 3, T])
        gate_bf = sb("gate_bf", [P, T], BF16)
        top_v = sb("top_v", [P, 2 * HEADS, TOPK])
        top_i = sb("top_i", [P, 2 * HEADS, TOPK], U32)
        top_f = sb("top_f", [P, 2 * HEADS, TOPK])
        cand = sb("cand", [P, HEADS, NCAND])
        cand2 = sb("cand2", [P, HEADS, NCAND])
        code = sb("code", [P, HEADS, NCAND])
        best_v = sb("best_v", [P, HEADS, TOPK])
        best_i = sb("best_i", [P, HEADS, TOPK], U32)
        best_f = sb("best_f", [P, HEADS, TOPK])
        best_e = sb("best_e", [P, HEADS, TOPK])
        expert = sb("expert", [P, HEADS * TOPK], I32)
        expert_i = sb("expert_i", [P, HEADS * TOPK], I32)
        expert_j = sb("expert_j", [P, HEADS * TOPK], I32)
        i_f = sb("i_f", [P, HEADS * TOPK])
        j_f = sb("j_f", [P, HEADS * TOPK])
        gate = sb("gate", [P, HEADS, TOPK])
        gate_z = sb("gate_z", [P, HEADS])
        cols = sb("cols", [P, NCOLS])
        c_act = sb("c_act", [P, KC])
        mod = sb("mod", [P, MOD_TILES])
        gain = sb("gain", [P, 4, KC])
        sk = sb("sk", [P, 2, 2, NK])
        ws = sb("ws", [P, AC, P])
        bs = sb("bs", [P, AC, P])
        ones = sb("ones", [P, P])
        ident = sb("ident", [P, P])
        iota_i = sb("iota_i", [P, P], I32)
        iota_bf = sb("iota_bf", [P, P], BF16)
        iota_f = sb("iota_f", [P, P])

        def part(at, *dims):
            n = int(np.prod(dims))
            v = shared[:, at:at + n]
            if len(dims) == 2:
                return v.rearrange("p (a b) -> p a b", a=dims[0])
            if len(dims) == 3:
                return v.rearrange("p (a b c) -> p a b c", a=dims[0], b=dims[1])
            return v

        sq = part(0, KC, T)
        PAD = TAPS - 1
        z = part(0, 4, T)
        a_pad = part(2048, AC, T + PAD + 2)
        conv = part(4224, AC, T)
        v_c = part(6272, AC, T)
        u_c = part(8320, AC, T)
        v_tok = part(10368, AC, T)
        ln_sq = part(12416, AC, T)
        zc = part(0, 4, T)
        m_pad = part(2048, 2, T + 4)
        y_c = part(4096, KC, T)
        q = part(0, Q_TILES, T)
        work = part(0, 2 * HEADS, NK)
        work2 = part(2048, 2 * HEADS, NK)
        pick = part(4096, TOPK, NCAND)
        scores = part(8192, TB, 2 * HEADS, NK)
        gate_st = part(0, 2, NK, HALF)
        g_ring = part(0, RING, T)
        prod = part(2048, 2, T)
        stat = act_ring

        ld = [sem(f"ld{i}") for i in range(RING)]
        act_st = [sem(f"act_st{i}") for i in range(RING)]
        act_ld = [sem(f"act_ld{i}") for i in range(RING)]
        g_ld = [sem(f"g_ld{i}") for i in range(RING)]
        g_st = [sem(f"g_st{i}") for i in range(2)]
        names = ("inputs consts mod_done c_ready mod_ready hi_ready lo_ready tile_done evac hh_ready hl_ready "
                 "x_ready sq_ready ssum var_ready sd_ready t_ready glu_done act_chain dve_chain pool_chain "
                 "ln_mm ln_sqd ln_var ln_sd ln_t ln_out v_tr v_tok_ready mixed mixed_read bout "
                 "top_step out_ready stored sc_mm sc_ev topk exp_in exp_out tr_mm tr_read "
                 "oh_ready g_mm g_ev p_ready ph_ready pl_ready z_free").split()
        S = {n: sem(n) for n in names}

        def col(name, i):
            return cols[:, COLS[name] + i:COLS[name] + i + 1]

        def modc(l, which, k):
            i = l * 6 * KC + which * KC + k
            return mod[:, i:i + 1]

        block = ctx.enter_context(nc.Block())

        @block.sync
        def _(sp):
            sp.dma_start(cols[:], cols_in).then_inc(S["inputs"], 16)
            sp.dma_start(sk[:], sk_in).then_inc(S["inputs"], 16)
            sp.dma_start(ws[:], ws_in).then_inc(S["inputs"], 16)
            sp.dma_start(bs[:], bs_in).then_inc(S["inputs"], 16)
            sp.dma_start(x[:], x_in).then_inc(S["inputs"], 16)

            def load_mod(grp, s, wait):
                if wait:
                    sp.wait_ge(S["mod_done"], grp * RING + s - RING + 1)
                sp.dma_start(w_raw[:, s, :], mod_stream[grp * RING + s]).then_inc(ld[s], 16)

            for s in range(RING):
                load_mod(0, s, False)
            with sp.Fori(1, MOD_TILES // RING) as i:
                for s in range(RING):
                    load_mod(i, s, True)

            def load(grp, s):
                sp.wait_ge(S["hi_ready"], grp * RING + s - RING + 1)
                sp.wait_ge(S["lo_ready"], grp * RING + s - RING + 1)
                sp.dma_start(w_raw[:, s, :], stream[grp * RING + s]).then_inc(ld[s], 16)

            for s in range(RING):
                sp.wait_ge(S["mod_done"], MOD_TILES - RING + s + 1)
                sp.dma_start(w_raw[:, s, :], stream[s]).then_inc(ld[s], 16)

            at = 1
            for l in range(2):
                first = BASE[f"v{l}"] // RING
                with sp.Fori(at, first) as i:
                    for s in range(RING):
                        load(i, s)

                def load_products(j4, s):
                    sp.dma_start(act_ring[:, s, :], act_dram[j4 * RING + s]).then_inc(act_ld[s], 16)
                    sp.dma_start(g_ring[:, s, :].rearrange("p (b t) -> p b t", t=HALF),
                                 gate_dram[:, :, j4 * RING + s, :].rearrange("b p t -> p b t")
                                 ).then_inc(g_ld[s], 16)

                for s in range(RING):
                    load(first, s)
                for r in range(RING):
                    sp.wait_ge(act_st[r], 16 * (l + 1) * EXPERT_TILES // RING)
                for r in range(2):
                    sp.wait_ge(g_st[r], 16 * ((l + 1) * T // HALF // 2 + 1))
                for s in range(RING):
                    load_products(0, s)
                with sp.Fori(1, EXPERT_TILES // RING) as i:
                    for s in range(RING):
                        load(i + first, s)
                        sp.wait_ge(S["p_ready"], i * RING + (l * EXPERT_TILES + s - RING + 1))
                        load_products(i, s)
                at = first + EXPERT_TILES // RING
            for k in range(KC):
                sp.wait_ge(S["out_ready"], k + 1)
                sp.dma_start(out[:, k, :], sq[:, k, :]).then_inc(S["stored"], 16)
            sp.wait_ge(S["stored"], 16 * KC)

        @block.gpsimd
        def _(pool):
            nc.gpsimd.memset(ones[:], 1.0)
            nc.gpsimd.iota(iota_i[:], [[1, P]], base=0, channel_multiplier=0)
            nc.gpsimd.memset(ident[:], 0.0).then_inc(S["pool_chain"], 1)
            pool.wait_ge(S["pool_chain"], 1)
            nc.gpsimd.affine_select(out=ident[:], in_=ident[:], compare_op=ALU.not_equal, fill=1.0, base=0,
                                    pattern=[[-1, P]], channel_multiplier=1)
            pool.wait_ge(S["inputs"], 80)
            nc.gpsimd.affine_select(out=ws[:], in_=ws[:], compare_op=ALU.is_ge, fill=0.0, base=0,
                                    pattern=[[0, AC], [1, P]], channel_multiplier=-1).then_inc(S["consts"], 1)
            with pool.Fori(0, TILES // RING) as i:
                for s in range(RING):
                    pool.wait_ge(S["hi_ready"], i * RING + s + 1)
                    nc.gpsimd.tensor_tensor(w_lo[:, s % 2, :], w_raw[:, s, :], w_hi[:, s % 2, :].bitcast(F32),
                                            ALU.subtract).then_inc(S["lo_ready"], 1)

        @block.scalar
        def _(act):
            chain = [0]

            def link(ins):
                chain[0] += 1
                ins.then_inc(S["act_chain"], 1)
                act.wait_ge(S["act_chain"], chain[0])

            def make_hi(grp, s, first=False):
                grp, s = grp + s // RING, s % RING
                act.wait_ge(ld[s], (grp + MOD_TILES // RING) * 16 + 16)
                if not first:
                    act.wait_ge(S["tile_done"], grp * RING + s - 1)
                nc.scalar.activation(w_hi[:, s % 2, :], w_raw[:, s, :], ACT.Copy).then_inc(S["hi_ready"], 1)

            def evacuate(grp, s, dst, func, bank, **kw):
                act.wait_ge(S["tile_done"], grp * RING + s + 1)
                nc.scalar.activation(dst, ps[bank][:], func, **kw).then_inc(S["evac"], 1)

            def step(g, dst, func, **kw):
                evacuate(g // RING, g % RING, dst, func, g % 2, **kw)
                make_hi(g // RING, g % RING + 2)

            def norm_act(n, shift):
                act.wait_ge(S["x_ready"], XR[n])
                for k in range(KC):
                    nc.scalar.activation(sq[:, k, :], x[:, k, :], ACT.Square).then_inc(S["sq_ready"], 1)
                act.wait_ge(S["var_ready"], n + 1)
                nc.scalar.activation(stat[:, 1, :], stat[:, 0, :], ACT.Sqrt).then_inc(S["sd_ready"], 1)
                if shift is None:
                    return
                for k in range(KC):
                    act.wait_ge(S["t_ready"], n * KC + k + 1)
                    nc.scalar.activation(h_hi[:, k, :], sq[:, k, :], ACT.Identity, bias=shift(k)
                                         ).then_inc(S["hh_ready"], 1)

            def ln_act(m, src, finish):
                act.wait_ge(S["ln_t"], 2 * m + 1)
                for c in range(AC):
                    ins = nc.scalar.activation(ln_sq[:, c, :], src[:, c, :], ACT.Square)
                ins.then_inc(S["ln_sqd"], 1)
                act.wait_ge(S["ln_var"], m + 1)
                nc.scalar.activation(stat[:, 1, :], stat[:, 0, :], ACT.Sqrt).then_inc(S["ln_sd"], 1)
                act.wait_ge(S["ln_t"], 2 * m + 2)
                finish()

            def residual_act(name, l):
                base = BASE[name]
                for k in range(KC):
                    if k >= 2:
                        act.wait_ge(S["x_ready"], XR[{"ev_out": 0, "od_out": 2}[name]] + k - 1)
                    step(base + k, z[:, k % 2, :], ACT.Identity, scale=modc(l, 2, k))

            def peer_act(l):
                base = BASE[f"q{l}"]
                for i in range(Q_TILES):
                    step(base + i, q[:, i, :], ACT.Copy)
                for grp in range(TB * 4):
                    act.wait_ge(S["sc_mm"], l * TB * 4 + grp + 1)
                    nc.scalar.copy(scores[:, grp // 4, 4 * (grp % 4):4 * (grp % 4) + 4, :],
                                   ps[2 + grp % 2][:].rearrange("p (a b) -> p a b", a=4)
                                   ).then_inc(S["sc_ev"], 1)
                first = BASE[f"u{l}"] // RING

                def expert_step(grp, s):
                    rounds = grp + l * EXPERT_TILES // RING
                    if not (isinstance(grp, int) and grp == 0 and l == 0):
                        act.wait_ge(act_st[s], rounds * 16)
                    evacuate(grp + first, s, act_ring[:, s, :], ACT.Gelu, s % 2)
                    make_hi(grp + first, s + 2)
                    act.wait_ge(S["evac"], EVAC[f"u{l}"] + grp * RING + s + 1)
                    act.dma_start(act_dram[grp * RING + s], act_ring[:, s, :]).then_inc(act_st[s], 16)

                per = TILES_PER_BLOCK // RING

                def block_steps(b, skip=0):
                    for r in range(skip, per):
                        if r == per - 1:
                            act.wait_ge(S["exp_in"], l * TB + b + 1)
                            nc.scalar.activation(gate[:], best_v[:], ACT.Exp).then_inc(S["exp_out"], 1)
                        for s in range(RING):
                            expert_step(b * per + r, s)

                for s in range(RING):
                    expert_step(0, s)
                block_steps(0, 1)
                with act.Fori(1, TB) as b:
                    block_steps(b)
                at = TB * per
                with act.Fori(0, TB) as b:
                    for half in range(2):
                        act.wait_ge(g_st[half], b * 16 + (l * TB + 1) * 16)
                        with act.Fori(0, HALF // GROUP // RING) as r:
                            for s in range(RING):
                                expert_step(b * 4 + half * 2 + r + at, s)
                                for w in range(2):
                                    act.wait_ge(S["g_mm"], b * 32 + r * 8 + (l * 2 * T // GROUP + half * 16 + 2 * s + w + 1))
                                    nc.scalar.copy(
                                        gate_st[:, half, :, bass.ds(r * (RING * GROUP) + (s * GROUP + 4 * w), 4)]
                                        .rearrange("p j t -> p t j"),
                                        ps[2 + w][:].rearrange("p (t j) -> p t j", t=4)).then_inc(S["g_ev"], 1)
                        act.wait_ge(S["g_ev"], b * 32 + (l * 2 * T // GROUP + half * 16 + 16 + 2))
                        act.dma_start(gate_dram[b * 2 + half], gate_st[:, half, :, :]).then_inc(g_st[half], 16)
                at += T // GROUP // RING
                with act.Fori(at, EXPERT_TILES // RING) as i:
                    for s in range(RING):
                        expert_step(i, s)

                first = BASE[f"v{l}"] // RING

                def prod_hi(grp, s, head=False):
                    grp, s = grp + s // RING, s % RING
                    act.wait_ge(S["p_ready"], grp * RING + (l * EXPERT_TILES + s + 1))
                    if not head:
                        act.wait_ge(S["tile_done"], (grp + first) * RING + s - 1)
                    nc.scalar.activation(h_hi[:, s % 2, :], prod[:, s % 2, :], ACT.Copy).then_inc(S["ph_ready"], 1)

                prod_hi(0, 0, True)
                last = EXPERT_TILES // RING - 1
                with act.Fori(0, last) as i:
                    for s in range(RING):
                        prod_hi(i, s + 1)
                        make_hi(i + first, s + 2)
                for s in range(RING):
                    if s < RING - 1:
                        prod_hi(last, s + 1)
                    if (last + first) * RING + s + 2 < TILES:
                        make_hi(last + first, s + 2)

            for half in range(2):
                act.sem_inc(g_st[half], 16)
            act.sem_inc(S["g_ev"], 2)
            act.wait_ge(S["inputs"], 80)
            nc.scalar.activation(c_act[:], cols[:, COLS["c"]:COLS["c"] + KC], ACT.Silu).then_inc(S["c_ready"], 1)
            make_hi(0, 0, True)
            make_hi(0, 1, True)

            act.wait_ge(S["mod_ready"], 1)
            norm_act(0, lambda k: modc(0, 0, k))
            for c in range(AC):
                if c >= 2:
                    act.wait_ge(S["glu_done"], c - 1)
                step(2 * c, z[:, 2 * (c % 2), :], ACT.Copy)
                step(2 * c + 1, z[:, 2 * (c % 2) + 1, :], ACT.Sigmoid)
            for c in range(AC):
                step(8 + c, v_c[:, c, :], ACT.Gelu)
            for c in range(AC):
                step(12 + c, u_c[:, c, :], ACT.Gelu)

            def finish_v():
                for c in range(AC):
                    nc.scalar.activation(v_c[:, c, :], v_c[:, c, :], ACT.Identity, bias=col("gln_b", c)
                                         ).then_inc(S["ln_out"], 1)
                for c in range(AC):
                    act.wait_ge(S["v_tr"], c + 1)
                    nc.scalar.copy(v_tok[:, c, :], ps[2 + c % 2][:]).then_inc(S["v_tok_ready"], 1)

            def finish_a():
                for c in range(AC):
                    ins = nc.scalar.activation(conv[:, c, :], conv[:, c, :], ACT.Silu, bias=col("cln_b", c))
                link(ins)
                for c in range(AC):
                    nc.scalar.activation(h_hi[:, c, :], conv[:, c, :], ACT.Copy).then_inc(S["hh_ready"], 1)
                for c in range(AC):
                    act.wait_ge(S["bout"], c + 1)
                    nc.scalar.activation(h_hi[:, AC + c, :], u_c[:, c, :], ACT.Copy).then_inc(S["hh_ready"], 1)

            ln_act(0, v_c, finish_v)
            ln_act(1, conv, finish_a)
            residual_act("ev_out", 0)
            norm_act(1, lambda k: modc(0, 3, k))
            peer_act(0)

            norm_act(2, lambda k: modc(1, 0, k))
            for c in range(KC):
                g = BASE["od_in"] + 3 * c
                if c >= 1:
                    act.wait_ge(S["z_free"], c)
                for w in range(3):
                    evacuate((g + w) // RING, (g + w) % RING, zc[:, w, :], ACT.Copy, (g + w) % 2)
                    make_hi((g + w) // RING, (g + w) % RING + 2)
            for c in range(KC):
                act.wait_ge(S["z_free"], c + 1)
                nc.scalar.activation(h_hi[:, c, :], y_c[:, c, :], ACT.Copy).then_inc(S["hh_ready"], 1)
            residual_act("od_out", 1)
            norm_act(3, lambda k: modc(1, 3, k))
            peer_act(1)
            norm_act(4, None)

        @block.vector
        def _(dve):
            chain = [0]

            def link(ins, plus=0):
                chain[0] += 1
                ins.then_inc(S["dve_chain"], 1)
                dve.wait_ge(S["dve_chain"], plus + chain[0])

            V = nc.vector

            def inverse_root():
                link(V.reciprocal(stat[:, 2, :], stat[:, 1, :]))
                link(V.tensor_tensor(stat[:, 3, :], stat[:, 2, :], stat[:, 2, :], ALU.mult))
                link(V.tensor_tensor(stat[:, 3, :], stat[:, 3, :], stat[:, 0, :], ALU.mult))
                link(V.tensor_scalar(stat[:, 3, :], stat[:, 3, :], -0.5, 1.5, ALU.mult, ALU.add))
                link(V.tensor_tensor(stat[:, 2, :], stat[:, 2, :], stat[:, 3, :], ALU.mult))

            def norm_dve(n, gain_col, shift):
                dve.wait_ge(S["ssum"], n + 1)
                V.tensor_scalar(stat[:, 0, :], ps[5][:], 1.0 / D, EPS, ALU.mult, ALU.add).then_inc(S["var_ready"], 1)
                dve.wait_ge(S["sd_ready"], n + 1)
                inverse_root()
                for k in range(KC):
                    ins = V.scalar_tensor_tensor(out=sq[:, k, :], in0=x[:, k, :], scalar=gain_col(k),
                                                 in1=stat[:, 2, :], op0=ALU.mult, op1=ALU.mult)
                    ins.then_inc(S["t_ready"] if shift else S["out_ready"], 1)
                if not shift:
                    return
                for k in range(KC):
                    dve.wait_ge(S["hh_ready"], HR[n] + k + 1)
                    V.scalar_tensor_tensor(out=h_lo[:, k, :], in0=sq[:, k, :], scalar=shift(k),
                                           in1=h_hi[:, k, :].bitcast(F32), op0=ALU.add, op1=ALU.subtract
                                           ).then_inc(S["hl_ready"], 1)

            def ln_dve(m, src, gain_name):
                dve.wait_ge(S["ln_mm"], 2 * m + 1)
                link(V.tensor_scalar(stat[:, 0, :], ps[4][:], 1.0 / (AC * P), None, ALU.mult))
                for c in range(AC):
                    ins = V.tensor_tensor(src[:, c, :], src[:, c, :], stat[:, 0, :], ALU.subtract)
                ins.then_inc(S["ln_t"], 1)
                dve.wait_ge(S["ln_mm"], 2 * m + 2)
                V.tensor_scalar(stat[:, 0, :], ps[4][:], 1.0 / (AC * P), EPS, ALU.mult, ALU.add
                                ).then_inc(S["ln_var"], 1)
                dve.wait_ge(S["ln_sd"], m + 1)
                inverse_root()
                for c in range(AC):
                    ins = V.scalar_tensor_tensor(out=src[:, c, :], in0=src[:, c, :], scalar=col(gain_name, c),
                                                 in1=stat[:, 2, :], op0=ALU.mult, op1=ALU.mult)
                ins.then_inc(S["ln_t"], 1)

            def residual_dve(name):
                for k in range(KC):
                    dve.wait_ge(S["evac"], EVAC[name] + k + 1)
                    V.tensor_tensor(x[:, k, :], x[:, k, :], z[:, k % 2, :], ALU.add).then_inc(S["x_ready"], 1)

            def peer_dve(l):
                LINKS = 20
                base = chain[0]
                with dve.Fori(0, TB) as b:
                    plus = b * LINKS

                    def chained(ins):
                        link(ins, plus)

                    def then_top(ins):
                        link(ins, plus)
                        dve.sem_inc(S["top_step"], 1)

                    dve.wait_ge(S["sc_ev"], b * 4 + (l * TB * 4 + 4))
                    if True:
                        dve.wait_ge(S["sc_ev"], (l + 1) * TB * 4)
                    then_top(V.tensor_copy(work[:], scores[:, bass.ds(b, 1), :, :].rearrange("p o a b -> p (o a) b")))
                    for hp in range(2 * HEADS):
                        ins = V.max(top_v[:, hp, 0:8], work[:, hp, :])
                    then_top(ins)
                    for hp in range(2 * HEADS):
                        V.max_index(top_i[:, hp, 0:8], top_v[:, hp, 0:8], work[:, hp, :])
                        ins = V.match_replace(work2[:, hp, :], top_v[:, hp, 0:8], work[:, hp, :], LOWEST)
                    then_top(ins)
                    for hp in range(2 * HEADS):
                        ins = V.max(top_v[:, hp, 8:16], work2[:, hp, :])
                    then_top(ins)
                    for hp in range(2 * HEADS):
                        ins = V.max_index(top_i[:, hp, 8:16], top_v[:, hp, 8:16], work2[:, hp, :])
                    then_top(ins)
                    chained(V.tensor_copy(top_f[:], top_i[:]))
                    f4 = top_f[:].rearrange("p (h two) k -> p h two k", two=2)
                    v4 = top_v[:].rearrange("p (h two) k -> p h two k", two=2)
                    chained(V.tensor_scalar(f4[:, :, 0, :], f4[:, :, 0, :], float(NK), None, ALU.mult))
                    for dst, src in ((cand, v4), (code, f4)):
                        for (a, n), o in zip(ROWS, OFFS):
                            V.tensor_tensor(dst[:, :, o:o + n], src[:, :, 1, 0:n],
                                            src[:, :, 0, a:a + 1].to_broadcast([P, HEADS, n]), ALU.add)
                        ins = V.tensor_tensor(dst[:, :, OFFS[-1]:], src[:, :, 0, 8:16],
                                              src[:, :, 1, 0:1].to_broadcast([P, HEADS, 8]), ALU.add)
                    then_top(ins)
                    for h in range(HEADS):
                        ins = V.max(best_v[:, h, 0:8], cand[:, h, :])
                    then_top(ins)
                    for h in range(HEADS):
                        V.max_index(best_i[:, h, 0:8], best_v[:, h, 0:8], cand[:, h, :])
                        ins = V.match_replace(cand2[:, h, :], best_v[:, h, 0:8], cand[:, h, :], LOWEST)
                    then_top(ins)
                    for h in range(HEADS):
                        ins = V.max(best_v[:, h, 8:16], cand2[:, h, :])
                    then_top(ins)
                    for h in range(HEADS):
                        ins = V.max_index(best_i[:, h, 8:16], best_v[:, h, 8:16], cand2[:, h, :])
                    then_top(ins)
                    chained(V.tensor_copy(best_f[:], best_i[:]))
                    chained(V.tensor_copy(gate_z[:], best_v[:, :, 0:1].rearrange("p h o -> p (h o)")))
                    V.tensor_tensor(best_v[:], best_v[:], gate_z[:].unsqueeze(2).to_broadcast([P, HEADS, TOPK]),
                                    ALU.subtract).then_inc(S["exp_in"], 1)
                    for h in range(HEADS):
                        V.tensor_tensor(pick[:], best_f[:, h, :].unsqueeze(2).to_broadcast([P, TOPK, NCAND]),
                                        iota_f[:, 0:NCAND].unsqueeze(1).to_broadcast([P, TOPK, NCAND]),
                                        ALU.is_equal).then_inc(S["topk"], 1)
                        dve.wait_ge(S["topk"], b * 24 + (l * TB * 24 + 3 * h + 1))
                        V.tensor_tensor(pick[:], pick[:], code[:, h, :].unsqueeze(1).to_broadcast([P, TOPK, NCAND]),
                                        ALU.mult).then_inc(S["topk"], 1)
                        dve.wait_ge(S["topk"], b * 24 + (l * TB * 24 + 3 * h + 2))
                        V.tensor_reduce(best_e[:, h, :], pick[:], AX_X, ALU.add).then_inc(S["topk"], 1)
                        dve.wait_ge(S["topk"], b * 24 + (l * TB * 24 + 3 * h + 3))
                    chained(V.tensor_copy(expert[:], best_e[:].rearrange("p h k -> p (h k)")))
                    V.tensor_scalar(expert_i[:], expert[:], 7, None, ALU.logical_shift_right)
                    chained(V.tensor_scalar(expert_j[:], expert[:], NK - 1, None, ALU.bitwise_and))
                    V.tensor_copy(i_f[:], expert_i[:])
                    chained(V.tensor_copy(j_f[:], expert_j[:]))
                    dve.wait_ge(S["exp_out"], b + (l * TB + 1))
                    chained(V.tensor_reduce(gate_z[:], gate[:], AX_X, ALU.add))
                    chained(V.reciprocal(gate_z[:], gate_z[:]))
                    V.tensor_tensor(gate[:], gate[:], gate_z[:].unsqueeze(2).to_broadcast([P, HEADS, TOPK]),
                                    ALU.mult).then_inc(S["tr_read"], 1)
                    dve.wait_ge(S["tr_mm"], b + (l * TB + 1))
                    V.tensor_copy(i_t[:, bass.ds(b * P, P)], ps[4][:, 0:P])
                    V.tensor_copy(j_t[:, bass.ds(b * P, P)], ps[4][:, P:2 * P])
                    chained(V.tensor_copy(gate_t[:, 2, bass.ds(b * P, P)], ps[4][:, 2 * P:3 * P]))
                    assert chain[0] - base == LINKS, chain[0] - base
                chain[0] = base + TB * LINKS
                for part_no in range(2):
                    link(V.tensor_copy(gate_bf[:], gate_t[:, 2, :]))
                    link(V.tensor_copy(gate_t[:, part_no, :], gate_bf[:]))
                    link(V.tensor_tensor(gate_t[:, 2, :], gate_t[:, 2, :], gate_t[:, part_no, :], ALU.subtract))
                groups = l * T // GROUP

                def one_hots(r, s, head):
                    if not head:
                        dve.wait_ge(S["g_mm"], r * 4 + (2 * (groups + s) - 2))
                    for n in range(GROUP):
                        t = bass.ds(r * (2 * GROUP) + (s * GROUP + n), 1)
                        V.tensor_scalar(oh_i[:, s, n, :], iota_bf[:], i_t[:, t], None, ALU.is_equal)
                        for w in range(3):
                            ins = V.tensor_scalar(oh_j[:, s, n, w, :], iota_bf[:], j_t[:, t], gate_t[:, w, t],
                                                  ALU.is_equal, ALU.mult)
                    ins.then_inc(S["oh_ready"], 1)

                for s in range(2):
                    one_hots(0, s, l == 0)
                with dve.Fori(1, T // GROUP // 2) as r:
                    for s in range(2):
                        one_hots(r, s, False)

                first = BASE[f"v{l}"]

                def gated(grp, s, head=False):
                    grp, s = grp + s // RING, s % RING
                    dve.wait_ge(act_ld[s], grp * 16 + (l * EXPERT_TILES // RING + 1) * 16)
                    dve.wait_ge(g_ld[s], grp * 16 + (l * EXPERT_TILES // RING + 1) * 16)
                    if not head:
                        dve.wait_ge(S["pl_ready"], grp * RING + (l * EXPERT_TILES + s - 1))
                    V.tensor_tensor(prod[:, s % 2, :], act_ring[:, s, :], g_ring[:, s, :], ALU.mult
                                    ).then_inc(S["p_ready"], 1)

                def prod_lo(grp, s):
                    dve.wait_ge(S["ph_ready"], grp * RING + (l * EXPERT_TILES + s + 1))
                    V.tensor_tensor(h_lo[:, s % 2, :], prod[:, s % 2, :], h_hi[:, s % 2, :].bitcast(F32),
                                    ALU.subtract).then_inc(S["pl_ready"], 1)

                gated(0, 0, True)
                gated(0, 1, True)
                last = EXPERT_TILES // RING - 1
                with dve.Fori(0, last) as i:
                    for s in range(RING):
                        prod_lo(i, s)
                        gated(i, s + 2)
                for s in range(RING):
                    prod_lo(last, s)
                    if s < 2:
                        gated(last, s + 2)
                dve.wait_ge(S["tile_done"], first + EXPERT_TILES)
                for k in range(KC):
                    ins = V.scalar_tensor_tensor(out=x[:, k, :], in0=ps[k][:], scalar=modc(l, 5, k), in1=x[:, k, :],
                                                 op0=ALU.mult, op1=ALU.add)
                    ins.then_inc(S["x_ready"], 1)

            dve.wait_ge(S["consts"], 1)
            V.tensor_copy(iota_bf[:], iota_i[:])
            V.tensor_copy(iota_f[:], iota_i[:])
            dve.wait_ge(S["mod_done"], MOD_TILES)
            link(V.tensor_tensor(mod[:], ps[4][:, 0:MOD_TILES],
                                 cols[:, COLS["mod_b"]:COLS["mod_b"] + MOD_TILES], ALU.add))
            for n in range(4):
                l, which = n // 2, n % 2
                at = l * 6 * KC + (1 + 3 * which) * KC
                name = COLS[("norm1_g", "norm2_g")[which]] + l * KC
                ins = V.scalar_tensor_tensor(out=gain[:, n, :], in0=mod[:, at:at + KC], scalar=1.0,
                                             in1=cols[:, name:name + KC], op0=ALU.add, op1=ALU.mult)
            ins.then_inc(S["mod_ready"], 1)
            dve.wait_ge(S["mod_ready"], 1)

            norm_dve(0, lambda k: gain[:, 0, k:k + 1], lambda k: modc(0, 0, k))
            dve.wait_ge(S["hl_ready"], KC)
            V.memset(a_pad[:, :, 0:PAD], 0.0)
            for c in range(AC):
                dve.wait_ge(S["evac"], 2 * c + 2)
                V.tensor_tensor(a_pad[:, c, PAD:PAD + T], z[:, 2 * (c % 2), :], z[:, 2 * (c % 2) + 1, :], ALU.mult
                                ).then_inc(S["glu_done"], 1)
            dve.wait_ge(S["glu_done"], AC)
            for c in range(AC):
                ins = V.tensor_scalar(conv[:, c, :], a_pad[:, c, 0:T], col("conv_w", c * TAPS), col("conv_b", c),
                                      ALU.mult, ALU.add)
            link(ins)
            before = chain[0]
            with dve.Fori(1, TAPS) as tap:
                for c in range(AC):
                    ins = V.scalar_tensor_tensor(out=conv[:, c, :], in0=a_pad[:, c, bass.ds(tap, T)],
                                                 scalar=cols[:, bass.ds(tap + (COLS["conv_w"] + c * TAPS), 1)],
                                                 in1=conv[:, c, :], op0=ALU.mult, op1=ALU.add)
                ins.then_inc(S["dve_chain"], 1)
                dve.wait_ge(S["dve_chain"], tap + before)
            chain[0] = before + TAPS - 1
            ln_dve(0, v_c, "gln_g")
            ln_dve(1, conv, "cln_g")
            for c in range(AC):
                dve.wait_ge(S["mixed"], c + 1)
                V.tensor_tensor(z[:, c % 2, :].rearrange("p (n t) -> p n t", t=P),
                                ps[6 + c % 2][:].rearrange("p (n t) -> p n t", t=P),
                                bs[:, c:c + 1, :].to_broadcast([P, T // P, P]), ALU.add).then_inc(S["mixed_read"], 1)
                dve.wait_ge(S["mixed_read"], c + 1)
                V.tensor_tensor(u_c[:, c, :], u_c[:, c, :], z[:, c % 2, :], ALU.mult).then_inc(S["bout"], 1)
            for c in range(KC):
                dve.wait_ge(S["hh_ready"], KC + c + 1)
                src = conv[:, c, :] if c < AC else u_c[:, c - AC, :]
                V.tensor_tensor(h_lo[:, c, :], src, h_hi[:, c, :].bitcast(F32), ALU.subtract
                                ).then_inc(S["hl_ready"], 1)
            residual_dve("ev_out")
            norm_dve(1, lambda k: gain[:, 1, k:k + 1], lambda k: modc(0, 3, k))
            peer_dve(0)

            norm_dve(2, lambda k: gain[:, 2, k:k + 1], lambda k: modc(1, 0, k))
            dve.wait_ge(S["hl_ready"], HR[2] + KC)
            link(V.memset(m_pad[:, :, 0:2], 0.0))
            for c in range(KC):
                m = c % 2
                dve.wait_ge(S["evac"], EVAC["od_in"] + 3 * c + 3)
                link(V.tensor_tensor(m_pad[:, m, 2:2 + T], zc[:, 0, :], zc[:, 1, :], ALU.mult))
                link(V.tensor_scalar(y_c[:, c, :], m_pad[:, m, 0:T], col("od_conv_w", 3 * c), None, ALU.mult))
                for k in (1, 2):
                    link(V.scalar_tensor_tensor(out=y_c[:, c, :], in0=m_pad[:, m, k:k + T],
                                                scalar=col("od_conv_w", 3 * c + k), in1=y_c[:, c, :],
                                                op0=ALU.mult, op1=ALU.add))
                V.tensor_tensor(y_c[:, c, :], y_c[:, c, :], zc[:, 2, :], ALU.mult).then_inc(S["z_free"], 1)
            dve.wait_ge(S["z_free"], KC)
            for c in range(KC):
                dve.wait_ge(S["hh_ready"], 3 * KC + KC + c + 1)
                V.tensor_tensor(h_lo[:, c, :], y_c[:, c, :], h_hi[:, c, :].bitcast(F32), ALU.subtract
                                ).then_inc(S["hl_ready"], 1)
            residual_dve("od_out")
            norm_dve(3, lambda k: gain[:, 3, k:k + 1], lambda k: modc(1, 3, k))
            peer_dve(1)
            norm_dve(4, lambda k: col("final_g", k), None)

        @block.tensor
        def _(pe):
            MM = nc.tensor.matmul

            def operands_ready(grp, s):
                pe.wait_ge(S["hi_ready"], grp * RING + s + 1)
                pe.wait_ge(S["lo_ready"], grp * RING + s + 1)

            def project(grp, s, banked):
                operands_ready(grp, s)
                if banked is not None:
                    pe.wait_ge(S["evac"], banked - 1)
                o = ps[s % 2][:]
                for k in range(KC):
                    hi = w_hi[:, s % 2, k * P:(k + 1) * P]
                    lo = w_lo[:, s % 2, k * P:(k + 1) * P]
                    MM(o, hi, h_hi[:, k, :], start=(k == 0), stop=False)
                    MM(o, hi, h_lo[:, k, :], start=False, stop=False)
                    ins = MM(o, lo, h_hi[:, k, :], start=False, stop=(k == KC - 1))
                ins.then_inc(S["tile_done"], 1)

            def projections(name, n):
                g, b = BASE[name] // RING, EVAC[name]
                if b == 0:
                    for s in range(RING):
                        project(g, s, None if s < 2 else s)
                    g, b, n = g + 1, b + RING, n - RING
                with pe.Fori(0, n // RING) as i:
                    for s in range(RING):
                        project(i + g, s, i * RING + (b + s))

            def operand_built(r):
                pe.wait_ge(S["hh_ready"], (r + 1) * KC)
                pe.wait_ge(S["hl_ready"], (r + 1) * KC)

            def sum_squares(n):
                for k in range(KC):
                    pe.wait_ge(S["sq_ready"], n * KC + k + 1)
                    ins = MM(ps[5][:], ones[:], sq[:, k, :], start=(k == 0), stop=(k == KC - 1))
                ins.then_inc(S["ssum"], 1)

            def ln_sums(m, src):
                for c in range(AC):
                    ins = MM(ps[4][:], ones[:], src[:, c, :], start=(c == 0), stop=(c == AC - 1))
                ins.then_inc(S["ln_mm"], 1)
                pe.wait_ge(S["ln_sqd"], m + 1)
                for c in range(AC):
                    ins = MM(ps[4][:], ones[:], ln_sq[:, c, :], start=(c == 0), stop=(c == AC - 1))
                ins.then_inc(S["ln_mm"], 1)

            def peer_pe(l):
                projections(f"q{l}", Q_TILES)
                pe.wait_ge(S["evac"], EVAC[f"u{l}"])
                for grp in range(TB * 4):
                    b = grp // 4
                    if grp >= 2:
                        pe.wait_ge(S["sc_ev"], l * TB * 4 + grp - 1)
                    for w in range(4):
                        hp = 4 * (grp % 4) + w
                        ins = MM(ps[2 + grp % 2][:, w * NK:(w + 1) * NK], q[:, hp, b * P:(b + 1) * P],
                                 sk[:, l, hp % 2, :], start=True, stop=True)
                    ins.then_inc(S["sc_mm"], 1)
                first, banked = BASE[f"u{l}"] // RING, EVAC[f"u{l}"]
                per = TILES_PER_BLOCK // RING
                with pe.Fori(0, TB) as b:
                    with pe.Fori(0, per) as r:
                        for s in range(RING):
                            project(b * per + r + first, s, b * TILES_PER_BLOCK + r * RING + (banked + s))
                    pe.wait_ge(S["tr_read"], b + (l * TB + 1))
                    nc.tensor.transpose(ps[4][:, 0:P], i_f[:], ident[:])
                    nc.tensor.transpose(ps[4][:, P:2 * P], j_f[:], ident[:])
                    nc.tensor.transpose(ps[4][:, 2 * P:3 * P], gate[:].rearrange("p h k -> p (h k)"), ident[:]
                                        ).then_inc(S["tr_mm"], 1)
                at = TB * per
                groups = l * T // GROUP
                with pe.Fori(0, T // GROUP // RING) as r:
                    for s in range(RING):
                        project(r + (at + first), s, r * RING + (banked + at * RING + s))
                        pe.wait_ge(S["oh_ready"], r * RING + (groups + s + 1))
                        for w in range(2):
                            pe.wait_ge(S["g_ev"], r * 8 + (2 * groups + 2 * s + w + 1))
                            for n in range(4):
                                for p3 in range(3):
                                    ins = MM(ps[2 + w][:, n * NK:(n + 1) * NK], oh_i[:, s % 2, 4 * w + n, :],
                                             oh_j[:, s % 2, 4 * w + n, p3, :], start=(p3 == 0), stop=(p3 == 2))
                            ins.then_inc(S["g_mm"], 1)
                at += T // GROUP // RING
                with pe.Fori(0, EXPERT_TILES // RING - at) as i:
                    for s in range(RING):
                        project(i + (at + first), s, i * RING + (banked + at * RING + s))
                first = BASE[f"v{l}"] // RING
                pe.wait_ge(S["evac"], banked + EXPERT_TILES)
                pe.wait_ge(S["g_ev"], (l + 1) * 2 * T // GROUP + 2)

                def accumulate(grp, s, start, stop):
                    operands_ready(grp + first, s)
                    pe.wait_ge(S["ph_ready"], grp * RING + (l * EXPERT_TILES + s + 1))
                    pe.wait_ge(S["pl_ready"], grp * RING + (l * EXPERT_TILES + s + 1))
                    for k in range(KC):
                        hi = w_hi[:, s % 2, k * P:(k + 1) * P]
                        lo = w_lo[:, s % 2, k * P:(k + 1) * P]
                        MM(ps[k][:], hi, h_hi[:, s % 2, :], start=start, stop=False)
                        MM(ps[k][:], hi, h_lo[:, s % 2, :], start=False, stop=False)
                        ins = MM(ps[k][:], lo, h_hi[:, s % 2, :], start=False, stop=stop)
                    ins.then_inc(S["tile_done"], 1)

                last = EXPERT_TILES // RING - 1
                for s in range(RING):
                    accumulate(0, s, s == 0, False)
                with pe.Fori(1, last) as i:
                    for s in range(RING):
                        accumulate(i, s, False, False)
                for s in range(RING):
                    accumulate(last, s, False, s == RING - 1)

            pe.wait_ge(S["c_ready"], 1)
            with pe.Fori(0, MOD_TILES // RING) as i:
                for s in range(RING):
                    pe.wait_ge(ld[s], i * 16 + 16)
                    for k in range(KC):
                        ins = MM(ps[4][:, bass.ds(i * RING + s, 1)], w_raw[:, s, k * P:(k + 1) * P],
                                 c_act[:, k:k + 1], start=(k == 0), stop=(k == KC - 1))
                    ins.then_inc(S["mod_done"], 1)

            pe.wait_ge(S["consts"], 1)
            sum_squares(0)
            operand_built(0)
            projections("ev_in", EV_IN)
            pe.wait_ge(S["evac"], EV_IN)
            ln_sums(0, v_c)
            for c in range(AC):
                pe.wait_ge(S["ln_out"], c + 1)
                if c >= 2:
                    pe.wait_ge(S["v_tok_ready"], c - 1)
                for n in range(T // P):
                    ins = nc.tensor.transpose(ps[2 + c % 2][:, n * P:(n + 1) * P], v_c[:, c, n * P:(n + 1) * P],
                                              ident[:])
                ins.then_inc(S["v_tr"], 1)
            ln_sums(1, conv)
            for c in range(AC):
                pe.wait_ge(S["v_tok_ready"], c + 1)
                if c >= 2:
                    pe.wait_ge(S["mixed_read"], c - 1)
                for n in range(T // P):
                    ins = MM(ps[6 + c % 2][:, n * P:(n + 1) * P], v_tok[:, c, n * P:(n + 1) * P], ws[:, c, :],
                             start=True, stop=True)
                ins.then_inc(S["mixed"], 1)
            operand_built(1)
            projections("ev_out", EV_OUT)
            sum_squares(1)
            operand_built(2)
            peer_pe(0)
            sum_squares(2)
            operand_built(3)
            projections("od_in", OD_IN)
            operand_built(4)
            projections("od_out", OD_OUT)
            sum_squares(3)
            operand_built(5)
            peer_pe(1)
            sum_squares(4)


XR = [0, KC, 2 * KC, 3 * KC, 4 * KC]
HR = [0, 2 * KC, 3 * KC, 5 * KC, 6 * KC]


def kernel(**inputs):
    import concourse.bacc as bacc
    from concourse.bass_utils import run_bass_kernel_spmd

    a = {n: np.asarray(v) for n, v in inputs.items()}

    def tiles(w, order=None):
        t = w.reshape(KC, P, -1, P).transpose(2, 1, 0, 3)
        return t if order is None else t[order]

    ev_order = [i for c in range(AC) for i in (c, AC + c)] + [3 * AC + c for c in range(AC)] \
        + [2 * AC + c for c in range(AC)]
    od_order = [i for c in range(KC) for i in (KC + c, 2 * KC + c, c)]
    parts = []
    for l in range(2):
        if l == 0:
            parts += [tiles(a["ev_w_in"][0], ev_order), tiles(a["ev_w_out"][0])]
        else:
            parts += [tiles(a["od_w_in"][0], od_order), tiles(a["od_w_out"][0])]
        parts.append(tiles(a["pk_wq"][l]))
        parts.append(a["pk_u"][l].reshape(NK, NK, KC, P).transpose(1, 3, 2, 0))
        parts.append(a["pk_v"][l].reshape(NK, NK, D).transpose(1, 0, 2).reshape(NK, P, KC, P))
    stream = np.empty((TILES, P, D), a["x"].dtype)
    at = 0
    for p in parts:
        stream[at:at + len(p)].reshape(len(p), P, KC, P)[:] = p
        at += len(p)
    assert at == TILES
    mod_stream = np.concatenate([tiles(a["mod_w"][l]) for l in range(2)]).reshape(MOD_TILES, P, D)

    def columns(v):
        return v.reshape(-1, P).T

    cols = np.concatenate([
        columns(a["c"]), columns(a["mod_b"]), columns(a["norm1_g"]), columns(a["norm2_g"]),
        a["ev_conv_w"][0].reshape(TAPS, AC, P).transpose(2, 1, 0).reshape(P, AC * TAPS),
        columns(a["ev_conv_b"]), columns(a["ev_cln_g"]), columns(a["ev_cln_b"]), columns(a["ev_gln_g"]),
        columns(a["ev_gln_b"]), a["od_conv_w"][0].reshape(3, KC, P).transpose(2, 1, 0).reshape(P, 3 * KC),
        columns(a["final_g"])], axis=1)
    arrays = {
        "stream": stream,
        "mod_stream": mod_stream,
        "x_in": a["x"][0].T.reshape(KC, P, T).transpose(1, 0, 2),
        "cols_in": cols,
        "sk_in": a["pk_subkeys"].transpose(3, 0, 1, 2),
        "ws_in": a["ev_ws"][0].transpose(2, 0, 1),
        "bs_in": np.broadcast_to(a["ev_bs"][0][None], (P, AC, P)),
    }
    arrays = {n: np.ascontiguousarray(v) for n, v in arrays.items()}
    nc = bacc.Bacc("TRN2", target_bir_lowering=False, num_devices=1)
    args = {n: nc.dram_tensor(n, v.shape, mybir.dt.from_np(v.dtype), kind="ExternalInput").ap()
            for n, v in arrays.items()}
    out = nc.dram_tensor("out", [P, KC, T], F32, kind="ExternalOutput").ap()
    act_dram = nc.dram_tensor("act_dram", [EXPERT_TILES, P, T], F32).ap()
    gate_dram = nc.dram_tensor("gate_dram", [T // HALF, P, NK, HALF], F32).ap()
    build(nc, out=out, act_dram=act_dram, gate_dram=gate_dram, **args)
    r = run_bass_kernel_spmd(nc, [arrays], core_ids=[0])
    got = r.results[0]["out"]
    return np.ascontiguousarray(got.transpose(2, 1, 0).reshape(1, T, D))
```

```python
from contextlib import ExitStack

import numpy as np

import concourse.bass as bass
from concourse import mybir

F32 = mybir.dt.float32
F32R = mybir.dt.float32r
BF16 = mybir.dt.bfloat16
U32 = mybir.dt.uint32
I32 = mybir.dt.int32
ALU = mybir.AluOpType
ACT = mybir.ActivationFunctionType
AX_X = mybir.AxisListType.X

P = 128
D = 1024
KC = D // P
T = 512
EPS = 1e-6
AC = 512 // P
TAPS = 31
HEADS = 8
TOPK = 16
NK = 128
TB = T // P
LOWEST = -3.0e38

MOD = 2 * 6 * KC
MOD_A = 2 * KC
MOD_B = 4 * KC
MOD_C = 6 * KC
MOD_B_RING = 3
MOD_C_ROUNDS = MOD_C // 2
EV_IN, EV_OUT, OD_IN, OD_OUT = 16, KC, 3 * KC, KC
Q_TILES, EXPERT_TILES = 2 * HEADS, NK
BASE = {}
EVAC = {}
_g = _b = 0
for _name, _n, _banked in [("ev_in", EV_IN, 1), ("ev_out", EV_OUT, 1), ("q0", Q_TILES, 1), ("u0", EXPERT_TILES, 1),
                           ("v0", EXPERT_TILES, 0), ("od_in", OD_IN, 1), ("od_out", OD_OUT, 1), ("q1", Q_TILES, 1),
                           ("u1", EXPERT_TILES, 1), ("v1", EXPERT_TILES, 0)]:
    BASE[_name], EVAC[_name] = _g, _b
    _g += _n
    _b += _n * _banked
TILES = _g
RING = 4
assert all(b % RING == 0 for b in BASE.values()) and MOD_A % RING == 0

TILES_PER_BLOCK = 12
GROUP = 8
HALF = 64
TAIL_TILES = EXPERT_TILES - TB * TILES_PER_BLOCK - T // GROUP

ROWS = [(a, TOPK // (a + 1)) for a in range(TOPK // 2)]
OFFS = np.cumsum([0] + [n for _, n in ROWS]).tolist()
NCAND = OFFS[-1] + TOPK // 2

COLS = {}
_c = 0
for _name, _n in [("c", KC), ("mod_b", MOD), ("norm1_g", 2 * KC), ("norm2_g", 2 * KC), ("conv_w", AC * TAPS),
                  ("conv_b", AC), ("cln_g", AC), ("cln_b", AC), ("gln_g", AC), ("gln_b", AC),
                  ("od_conv_w", 3 * KC), ("final_g", KC)]:
    COLS[_name] = _c
    _c += _n
NCOLS = _c


def build(nc, stream, mod_rows, mod_cols, x_in, c_in, cols_in, sk_in, ws_in, bs_in, out, act_dram, gate_dram):
    with ExitStack() as ctx:
        def sb(name, shape, dt=F32):
            return ctx.enter_context(nc.sbuf_tensor(name, shape, dt))

        def sem(name):
            return ctx.enter_context(nc.semaphore(name))

        ps = [ctx.enter_context(nc.psum_tensor(f"bank{i}", [P, 512], F32)) for i in range(8)]

        x = sb("x", [P, KC, T])
        h_hi = sb("h_hi", [P, KC, T], F32R)
        h_lo = sb("h_lo", [P, KC, T], F32R)
        w_raw = sb("w_raw", [P, RING, D])
        w_hi = sb("w_hi", [P, 2, D], F32R)
        w_lo = sb("w_lo", [P, 2, D], F32R)
        shared = sb("shared", [P, 16384])
        oh_i = sb("oh_i", [P, 2, GROUP, NK], BF16)
        oh_j = sb("oh_j", [P, 2, GROUP, 3, NK], BF16)
        act_ring = sb("act_ring", [P, RING, T])
        i_t = sb("i_t", [P, T])
        j_t = sb("j_t", [P, T])
        gate_t = sb("gate_t", [P, 3, T])
        gate_bf = sb("gate_bf", [P, T], BF16)
        top_v = sb("top_v", [P, 2 * HEADS, TOPK])
        top_i = sb("top_i", [P, 2 * HEADS, TOPK], U32)
        top_f = sb("top_f", [P, 2 * HEADS, TOPK])
        cand = sb("cand", [P, HEADS, NCAND])
        cand2 = sb("cand2", [P, HEADS, NCAND])
        code = sb("code", [P, HEADS, NCAND])
        best_v = sb("best_v", [P, HEADS, TOPK])
        best_i = sb("best_i", [P, HEADS, TOPK], U32)
        best_f = sb("best_f", [P, HEADS, TOPK])
        best_e = sb("best_e", [P, HEADS, TOPK])
        expert = sb("expert", [P, HEADS * TOPK], I32)
        expert_i = sb("expert_i", [P, HEADS * TOPK], I32)
        expert_j = sb("expert_j", [P, HEADS * TOPK], I32)
        i_f = sb("i_f", [P, HEADS * TOPK])
        j_f = sb("j_f", [P, HEADS * TOPK])
        gate = sb("gate", [P, HEADS, TOPK])
        gate_z = sb("gate_z", [P, HEADS])
        cols = sb("cols", [P, NCOLS])
        c_act = sb("c_act", [P, KC])
        c_row = sb("c_row", [P, D])
        mod = sb("mod", [P, MOD])
        gain = sb("gain", [P, 4, KC])
        sk = sb("sk", [P, 2, 2, NK])
        ws = sb("ws", [P, AC, P])
        bs = sb("bs", [P, AC, P])
        ones = sb("ones", [P, P])
        ident = sb("ident", [P, P])
        iota_i = sb("iota_i", [P, P], I32)
        iota_bf = sb("iota_bf", [P, P], BF16)
        iota_f = sb("iota_f", [P, P])

        def part(at, *dims):
            n = int(np.prod(dims))
            v = shared[:, at:at + n]
            if len(dims) == 2:
                return v.rearrange("p (a b) -> p a b", a=dims[0])
            if len(dims) == 3:
                return v.rearrange("p (a b c) -> p a b c", a=dims[0], b=dims[1])
            return v

        sq = part(0, KC, T)
        PAD = TAPS - 1
        z = part(0, 4, T)
        a_pad = part(2048, AC, T + PAD + 2)
        conv = part(4224, AC, T)
        v_c = part(6272, AC, T)
        u_c = part(8320, AC, T)
        v_tok = part(10368, AC, T)
        ln_sq = part(12416, AC, T)
        zc = part(0, 4, T)
        m_pad = part(2048, 2, T + 4)
        y_c = part(4096, KC, T)
        y_slot = part(12416, 2, T)
        q = part(0, Q_TILES, T)
        work = part(0, 2 * HEADS, NK)
        work2 = part(2048, 2 * HEADS, NK)
        pick = part(4096, TOPK, NCAND)
        scores = part(8192, TB, 2 * HEADS, NK)
        gate_st = part(0, 2, NK, HALF)
        g_ring = part(0, RING, T)
        prod = part(2048, 2, T)
        mod_c_ring = part(4096, 2, D)
        mod_b_ring = oh_j[:].rearrange("p a b c d -> p (a b c d)").bitcast(F32).rearrange("p (a b) -> p a b", b=D)
        stat = act_ring

        ld = [sem(f"ld{i}") for i in range(RING)]
        act_st = [sem(f"act_st{i}") for i in range(RING)]
        act_ld = [sem(f"act_ld{i}") for i in range(RING)]
        g_ld = [sem(f"g_ld{i}") for i in range(RING)]
        mod_b_ld = [sem(f"mod_b_ld{i}") for i in range(MOD_B_RING)]
        mod_c_ld = [sem(f"mod_c_ld{i}") for i in range(2)]
        g_st = [sem(f"g_st{i}") for i in range(2)]
        names = ("inputs c_in consts mod_a_done mod_b_done mod_c_done c_ready mod_ready hi_ready lo_ready tile_done evac hh_ready hl_ready "
                 "x_ready sq_ready ssum var_ready sd_ready t_ready glu_done act_chain dve_chain pool_chain "
                 "ln_mm ln_sqd ln_var ln_sd ln_t ln_out v_tr v_tok_ready mixed mixed_read bout "
                 "top_step out_ready stored sc_mm sc_ev topk exp_in exp_out tr_mm tr_read "
                 "oh_ready g_mm g_ev p_ready ph_ready pl_ready z_free").split()
        S = {n: sem(n) for n in names}

        def col(name, i):
            return cols[:, COLS[name] + i:COLS[name] + i + 1]

        def modc(l, which, k):
            i = l * 6 * KC + which * KC + k
            return mod[:, i:i + 1]

        def out_bank(k):
            return ps[(k + 5) % 8][:]

        block = ctx.enter_context(nc.Block())

        @block.sync
        def _(sp):
            sp.dma_start(c_row[:], c_in).then_inc(S["c_in"], 16)

            def load_mod_a(grp, s, wait):
                if wait:
                    sp.wait_ge(S["mod_a_done"], grp * RING + s - RING + 1)
                sp.dma_start(w_raw[:, s, :], mod_rows[grp * RING + s]).then_inc(ld[s], 16)

            for s in range(RING):
                load_mod_a(0, s, False)
            with sp.Fori(1, MOD_A // RING) as i:
                for s in range(RING):
                    load_mod_a(i, s, True)

            def load(grp, s):
                sp.wait_ge(S["hi_ready"], grp * RING + s - RING + 1)
                sp.wait_ge(S["lo_ready"], grp * RING + s - RING + 1)
                sp.dma_start(w_raw[:, s, :], stream[grp * RING + s]).then_inc(ld[s], 16)

            for s in range(RING):
                sp.wait_ge(S["mod_a_done"], MOD_A - RING + s + 1)
                sp.dma_start(w_raw[:, s, :], stream[s]).then_inc(ld[s], 16)
            at = BASE["ev_out"] // RING + 1
            with sp.Fori(1, at) as i:
                for s in range(RING):
                    load(i, s)
            for s in range(MOD_B_RING):
                sp.dma_start(mod_b_ring[:, s, :], mod_cols[s]).then_inc(mod_b_ld[s], 16)
            for m in range(MOD_B_RING, MOD_B):
                s = m % MOD_B_RING
                sp.wait_ge(S["mod_b_done"], m - MOD_B_RING + 1)
                sp.dma_start(mod_b_ring[:, s, :], mod_cols[m]).then_inc(mod_b_ld[s], 16)

            for l in range(2):
                first = BASE[f"v{l}"] // RING
                with sp.Fori(at, first) as i:
                    for s in range(RING):
                        load(i, s)

                def load_products(j4, s):
                    sp.dma_start(act_ring[:, s, :], act_dram[j4 * RING + s]).then_inc(act_ld[s], 16)
                    sp.dma_start(g_ring[:, s, :].rearrange("p (b t) -> p b t", t=HALF),
                                 gate_dram[:, :, j4 * RING + s, :].rearrange("b p t -> p b t")
                                 ).then_inc(g_ld[s], 16)

                for s in range(RING):
                    load(first, s)
                for r in range(2):
                    sp.wait_ge(g_st[r], 16 * ((l + 1) * T // HALF // 2 + 1))
                for s in range(RING):
                    sp.wait_ge(act_st[s], 16 * (l + 1) * EXPERT_TILES // RING)
                    load_products(0, s)

                def expert_loads(i):
                    for s in range(RING):
                        load(i + first, s)
                        sp.wait_ge(S["p_ready"], i * RING + (l * EXPERT_TILES + s - RING + 1))
                        load_products(i, s)

                rounds = 0
                if l == 0:
                    rounds = MOD_C_ROUNDS
                    for s in range(2):
                        sp.dma_start(mod_c_ring[:, s, :], mod_rows[MOD_A + s]).then_inc(mod_c_ld[s], 16)
                    with sp.Fori(1, rounds) as i:
                        expert_loads(i)
                        for s in range(2):
                            sp.wait_ge(S["mod_c_done"], i * 2 + s - 1)
                            sp.dma_start(mod_c_ring[:, s, :], mod_rows[i * 2 + (MOD_A + s)]
                                         ).then_inc(mod_c_ld[s], 16)
                with sp.Fori(max(rounds, 1), EXPERT_TILES // RING) as i:
                    expert_loads(i)
                at = first + EXPERT_TILES // RING
            for k in range(KC):
                sp.wait_ge(S["out_ready"], k + 1)
                sp.dma_start(out[:, k, :], sq[:, k, :]).then_inc(S["stored"], 16)
            sp.wait_ge(S["stored"], 16 * KC)

        @block.gpsimd
        def _(pool):
            nc.gpsimd.memset(ones[:], 1.0)
            nc.gpsimd.iota(iota_i[:], [[1, P]], base=0, channel_multiplier=0)
            nc.gpsimd.memset(ident[:], 0.0).then_inc(S["pool_chain"], 1)
            pool.wait_ge(S["pool_chain"], 1)
            nc.gpsimd.affine_select(out=ident[:], in_=ident[:], compare_op=ALU.not_equal, fill=1.0, base=0,
                                    pattern=[[-1, P]], channel_multiplier=1)
            pool.wait_ge(S["inputs"], 16 * N_INPUTS)
            nc.gpsimd.affine_select(out=ws[:], in_=ws[:], compare_op=ALU.is_ge, fill=0.0, base=0,
                                    pattern=[[0, AC], [1, P]], channel_multiplier=-1).then_inc(S["consts"], 1)
            with pool.Fori(0, TILES // RING) as i:
                for s in range(RING):
                    pool.wait_ge(S["hi_ready"], i * RING + s + 1)
                    nc.gpsimd.tensor_tensor(w_lo[:, s % 2, :], w_raw[:, s, :], w_hi[:, s % 2, :].bitcast(F32),
                                            ALU.subtract).then_inc(S["lo_ready"], 1)

        @block.scalar
        def _(act):
            chain = [0]

            def link(ins):
                chain[0] += 1
                ins.then_inc(S["act_chain"], 1)
                act.wait_ge(S["act_chain"], chain[0])

            def make_hi(grp, s, first=False):
                grp, s = grp + s // RING, s % RING
                act.wait_ge(ld[s], (grp + MOD_A // RING) * 16 + 16)
                if not first:
                    act.wait_ge(S["tile_done"], grp * RING + s - 1)
                nc.scalar.activation(w_hi[:, s % 2, :], w_raw[:, s, :], ACT.Copy).then_inc(S["hi_ready"], 1)

            def evacuate(grp, s, dst, func, bank, **kw):
                act.wait_ge(S["tile_done"], grp * RING + s + 1)
                nc.scalar.activation(dst, ps[bank][:], func, **kw).then_inc(S["evac"], 1)

            def step(g, dst, func, **kw):
                evacuate(g // RING, g % RING, dst, func, g % 2, **kw)
                make_hi(g // RING, g % RING + 2)

            def square(k):
                nc.scalar.activation(sq[:, k, :], x[:, k, :], ACT.Square).then_inc(S["sq_ready"], 1)

            def norm_act(n, shift):
                if n not in RESIDUAL:
                    for k in range(KC):
                        if n:
                            act.wait_ge(S["x_ready"], XR[n] - KC + k + 1)
                        square(k)
                act.wait_ge(S["var_ready"], n + 1)
                nc.scalar.activation(stat[:, 1, :], stat[:, 0, :], ACT.Sqrt).then_inc(S["sd_ready"], 1)
                if shift is None:
                    return
                for k in range(KC):
                    act.wait_ge(S["t_ready"], n * KC + k + 1)
                    nc.scalar.activation(h_hi[:, k, :], sq[:, k, :], ACT.Identity, bias=shift(k)
                                         ).then_inc(S["hh_ready"], 1)

            def ln_act(m, src, finish):
                act.wait_ge(S["ln_t"], 2 * m + 1)
                for c in range(AC):
                    ins = nc.scalar.activation(ln_sq[:, c, :], src[:, c, :], ACT.Square)
                ins.then_inc(S["ln_sqd"], 1)
                act.wait_ge(S["ln_var"], m + 1)
                nc.scalar.activation(stat[:, 1, :], stat[:, 0, :], ACT.Sqrt).then_inc(S["ln_sd"], 1)
                act.wait_ge(S["ln_t"], 2 * m + 2)
                finish()

            def residual_act(name, l):
                base, had = BASE[name], XR[{"ev_out": 0, "od_out": 2}[name]]
                for k in range(KC):
                    step(base + k, y_slot[:, k % 2, :], ACT.Identity, scale=modc(l, 2, k))
                    if k:
                        act.wait_ge(S["x_ready"], had + k)
                        square(k - 1)
                act.wait_ge(S["x_ready"], had + KC)
                square(KC - 1)

            def peer_act(l):
                base = BASE[f"q{l}"]
                for i in range(Q_TILES):
                    step(base + i, q[:, i, :], ACT.Copy)
                for grp in range(TB * 4):
                    act.wait_ge(S["sc_mm"], l * TB * 4 + grp + 1)
                    nc.scalar.copy(scores[:, grp // 4, 4 * (grp % 4):4 * (grp % 4) + 4, :],
                                   ps[2 + grp % 2][:].rearrange("p (a b) -> p a b", a=4)
                                   ).then_inc(S["sc_ev"], 1)
                first = BASE[f"u{l}"] // RING

                def expert_step(grp, s):
                    rounds = grp + l * EXPERT_TILES // RING
                    if not (isinstance(grp, int) and grp == 0 and l == 0):
                        act.wait_ge(act_st[s], rounds * 16)
                    evacuate(grp + first, s, act_ring[:, s, :], ACT.Gelu, s % 2)
                    make_hi(grp + first, s + 2)
                    act.wait_ge(S["evac"], EVAC[f"u{l}"] + grp * RING + s + 1)
                    act.dma_start(act_dram[grp * RING + s], act_ring[:, s, :]).then_inc(act_st[s], 16)

                per = TILES_PER_BLOCK // RING

                def block_steps(b, skip=0):
                    for r in range(skip, per):
                        if r == per - 1:
                            act.wait_ge(S["exp_in"], l * TB + b + 1)
                            nc.scalar.activation(gate[:], best_v[:], ACT.Exp).then_inc(S["exp_out"], 1)
                        for s in range(RING):
                            expert_step(b * per + r, s)

                for s in range(RING):
                    expert_step(0, s)
                block_steps(0, 1)
                with act.Fori(1, TB) as b:
                    block_steps(b)
                at = TB * per
                with act.Fori(0, TB) as b:
                    for half in range(2):
                        act.wait_ge(g_st[half], b * 16 + (l * TB + 1) * 16)
                        with act.Fori(0, HALF // GROUP // RING) as r:
                            for s in range(RING):
                                expert_step(b * 4 + half * 2 + r + at, s)
                                for w in range(2):
                                    act.wait_ge(S["g_mm"], b * 32 + r * 8 + (l * 2 * T // GROUP + half * 16 + 2 * s + w + 1))
                                    nc.scalar.copy(
                                        gate_st[:, half, :, bass.ds(r * (RING * GROUP) + (s * GROUP + 4 * w), 4)]
                                        .rearrange("p j t -> p t j"),
                                        ps[2 + w][:].rearrange("p (t j) -> p t j", t=4)).then_inc(S["g_ev"], 1)
                        act.wait_ge(S["g_ev"], b * 32 + (l * 2 * T // GROUP + half * 16 + 16 + 2))
                        act.dma_start(gate_dram[b * 2 + half], gate_st[:, half, :, :]).then_inc(g_st[half], 16)
                at += T // GROUP // RING
                with act.Fori(at, EXPERT_TILES // RING) as i:
                    for s in range(RING):
                        expert_step(i, s)

                first = BASE[f"v{l}"] // RING

                def prod_hi(grp, s, head=False):
                    grp, s = grp + s // RING, s % RING
                    act.wait_ge(S["p_ready"], grp * RING + (l * EXPERT_TILES + s + 1))
                    if not head:
                        act.wait_ge(S["tile_done"], (grp + first) * RING + s - 1)
                    nc.scalar.activation(h_hi[:, s % 2, :], prod[:, s % 2, :], ACT.Copy).then_inc(S["ph_ready"], 1)

                prod_hi(0, 0, True)
                last = EXPERT_TILES // RING - 1
                with act.Fori(0, last) as i:
                    for s in range(RING):
                        prod_hi(i, s + 1)
                        make_hi(i + first, s + 2)
                for s in range(RING):
                    if s < RING - 1:
                        prod_hi(last, s + 1)
                    if (last + first) * RING + s + 2 < TILES:
                        make_hi(last + first, s + 2)

            act.dma_start(cols[:], cols_in).then_inc(S["inputs"], 16)
            act.dma_start(x[:], x_in).then_inc(S["inputs"], 16)
            act.dma_start(sk[:], sk_in).then_inc(S["inputs"], 16)
            act.dma_start(ws[:], ws_in).then_inc(S["inputs"], 16)
            act.dma_start(bs[:], bs_in).then_inc(S["inputs"], 16)
            for half in range(2):
                act.sem_inc(g_st[half], 16)
            act.sem_inc(S["g_ev"], 2)
            act.wait_ge(S["c_in"], 16)
            nc.scalar.activation(c_row[:], c_row[:], ACT.Silu).then_inc(S["c_ready"], 1)
            act.wait_ge(S["inputs"], 16 * N_INPUTS)
            nc.scalar.activation(c_act[:], cols[:, COLS["c"]:COLS["c"] + KC], ACT.Silu).then_inc(S["c_ready"], 1)

            norm_act(0, lambda k: modc(0, 0, k))
            make_hi(0, 0, True)
            make_hi(0, 1, True)
            for c in range(AC):
                if c >= 2:
                    act.wait_ge(S["glu_done"], c - 1)
                step(2 * c, z[:, 2 * (c % 2), :], ACT.Copy)
                step(2 * c + 1, z[:, 2 * (c % 2) + 1, :], ACT.Sigmoid)
            for c in range(AC):
                step(8 + c, v_c[:, c, :], ACT.Gelu)
            for c in range(AC):
                step(12 + c, u_c[:, c, :], ACT.Gelu)

            def finish_v():
                for c in range(AC):
                    nc.scalar.activation(v_c[:, c, :], v_c[:, c, :], ACT.Identity, bias=col("gln_b", c)
                                         ).then_inc(S["ln_out"], 1)
                for c in range(AC):
                    act.wait_ge(S["v_tr"], c + 1)
                    nc.scalar.copy(v_tok[:, c, :], ps[2 + c % 2][:]).then_inc(S["v_tok_ready"], 1)

            def finish_a():
                for c in range(AC):
                    ins = nc.scalar.activation(conv[:, c, :], conv[:, c, :], ACT.Silu, bias=col("cln_b", c))
                link(ins)
                for c in range(AC):
                    nc.scalar.activation(h_hi[:, c, :], conv[:, c, :], ACT.Copy).then_inc(S["hh_ready"], 1)
                for c in range(AC):
                    act.wait_ge(S["bout"], c + 1)
                    nc.scalar.activation(h_hi[:, AC + c, :], u_c[:, c, :], ACT.Copy).then_inc(S["hh_ready"], 1)

            ln_act(0, v_c, finish_v)
            ln_act(1, conv, finish_a)
            act.wait_ge(S["mod_ready"], 2)
            residual_act("ev_out", 0)
            norm_act(1, lambda k: modc(0, 3, k))
            peer_act(0)

            norm_act(2, lambda k: modc(1, 0, k))
            for c in range(KC):
                g = BASE["od_in"] + 3 * c
                if c >= 1:
                    act.wait_ge(S["z_free"], c)
                for w in range(3):
                    evacuate((g + w) // RING, (g + w) % RING, zc[:, w, :], ACT.Copy, (g + w) % 2)
                    make_hi((g + w) // RING, (g + w) % RING + 2)
            for c in range(KC):
                act.wait_ge(S["z_free"], c + 1)
                nc.scalar.activation(h_hi[:, c, :], y_c[:, c, :], ACT.Copy).then_inc(S["hh_ready"], 1)
            residual_act("od_out", 1)
            norm_act(3, lambda k: modc(1, 3, k))
            peer_act(1)
            norm_act(4, None)

        @block.vector
        def _(dve):
            chain = [0]

            def link(ins, plus=0):
                chain[0] += 1
                ins.then_inc(S["dve_chain"], 1)
                dve.wait_ge(S["dve_chain"], plus + chain[0])

            V = nc.vector

            def inverse_root():
                link(V.reciprocal(stat[:, 2, :], stat[:, 1, :]))
                link(V.tensor_tensor(stat[:, 3, :], stat[:, 2, :], stat[:, 2, :], ALU.mult))
                link(V.tensor_tensor(stat[:, 3, :], stat[:, 3, :], stat[:, 0, :], ALU.mult))
                link(V.tensor_scalar(stat[:, 3, :], stat[:, 3, :], -0.5, 1.5, ALU.mult, ALU.add))
                link(V.tensor_tensor(stat[:, 2, :], stat[:, 2, :], stat[:, 3, :], ALU.mult))

            def norm_dve(n, gain_col, shift):
                dve.wait_ge(S["ssum"], n + 1)
                V.tensor_scalar(stat[:, 0, :], ps[5][:], 1.0 / D, EPS, ALU.mult, ALU.add).then_inc(S["var_ready"], 1)
                dve.wait_ge(S["sd_ready"], n + 1)
                inverse_root()
                for k in range(KC + 2):
                    if k < KC:
                        V.scalar_tensor_tensor(out=sq[:, k, :], in0=x[:, k, :], scalar=gain_col(k),
                                               in1=stat[:, 2, :], op0=ALU.mult, op1=ALU.mult
                                               ).then_inc(S["t_ready"] if shift else S["out_ready"], 1)
                    if k >= 2 and shift:
                        c = k - 2
                        dve.wait_ge(S["hh_ready"], HR[n] + c + 1)
                        V.scalar_tensor_tensor(out=h_lo[:, c, :], in0=sq[:, c, :], scalar=shift(c),
                                               in1=h_hi[:, c, :].bitcast(F32), op0=ALU.add, op1=ALU.subtract
                                               ).then_inc(S["hl_ready"], 1)

            def ln_centre(m, src):
                dve.wait_ge(S["ln_mm"], 2 * m + 1)
                link(V.tensor_scalar(stat[:, 0, :], ps[4][:], 1.0 / (AC * P), None, ALU.mult))
                for c in range(AC):
                    ins = V.tensor_tensor(src[:, c, :], src[:, c, :], stat[:, 0, :], ALU.subtract)
                ins.then_inc(S["ln_t"], 1)

            def ln_scale(m, src, gain_name):
                dve.wait_ge(S["ln_t"], 2 * m + 1)
                dve.wait_ge(S["ln_mm"], 2 * m + 2)
                V.tensor_scalar(stat[:, 0, :], ps[4][:], 1.0 / (AC * P), EPS, ALU.mult, ALU.add
                                ).then_inc(S["ln_var"], 1)
                dve.wait_ge(S["ln_sd"], m + 1)
                inverse_root()
                for c in range(AC):
                    ins = V.scalar_tensor_tensor(out=src[:, c, :], in0=src[:, c, :], scalar=col(gain_name, c),
                                                 in1=stat[:, 2, :], op0=ALU.mult, op1=ALU.mult)
                ins.then_inc(S["ln_t"], 1)

            def residual_dve(name):
                for k in range(KC):
                    dve.wait_ge(S["evac"], EVAC[name] + k + 1)
                    V.tensor_tensor(x[:, k, :], x[:, k, :], y_slot[:, k % 2, :], ALU.add).then_inc(S["x_ready"], 1)

            def peer_dve(l):
                LINKS = 20
                base = chain[0]
                with dve.Fori(0, TB) as b:
                    plus = b * LINKS

                    def chained(ins):
                        link(ins, plus)

                    def then_top(ins):
                        link(ins, plus)
                        dve.sem_inc(S["top_step"], 1)

                    dve.wait_ge(S["sc_ev"], b * 4 + (l * TB * 4 + 4))
                    if True:
                        dve.wait_ge(S["sc_ev"], (l + 1) * TB * 4)
                    then_top(V.tensor_copy(work[:], scores[:, bass.ds(b, 1), :, :].rearrange("p o a b -> p (o a) b")))
                    for hp in range(2 * HEADS):
                        ins = V.max(top_v[:, hp, 0:8], work[:, hp, :])
                    then_top(ins)
                    for hp in range(2 * HEADS):
                        V.max_index(top_i[:, hp, 0:8], top_v[:, hp, 0:8], work[:, hp, :])
                        ins = V.match_replace(work2[:, hp, :], top_v[:, hp, 0:8], work[:, hp, :], LOWEST)
                    then_top(ins)
                    for hp in range(2 * HEADS):
                        ins = V.max(top_v[:, hp, 8:16], work2[:, hp, :])
                    then_top(ins)
                    for hp in range(2 * HEADS):
                        ins = V.max_index(top_i[:, hp, 8:16], top_v[:, hp, 8:16], work2[:, hp, :])
                    then_top(ins)
                    chained(V.tensor_copy(top_f[:], top_i[:]))
                    f4 = top_f[:].rearrange("p (h two) k -> p h two k", two=2)
                    v4 = top_v[:].rearrange("p (h two) k -> p h two k", two=2)
                    chained(V.tensor_scalar(f4[:, :, 0, :], f4[:, :, 0, :], float(NK), None, ALU.mult))
                    for dst, src in ((cand, v4), (code, f4)):
                        for (a, n), o in zip(ROWS, OFFS):
                            V.tensor_tensor(dst[:, :, o:o + n], src[:, :, 1, 0:n],
                                            src[:, :, 0, a:a + 1].to_broadcast([P, HEADS, n]), ALU.add)
                        ins = V.tensor_tensor(dst[:, :, OFFS[-1]:], src[:, :, 0, 8:16],
                                              src[:, :, 1, 0:1].to_broadcast([P, HEADS, 8]), ALU.add)
                    then_top(ins)
                    for h in range(HEADS):
                        ins = V.max(best_v[:, h, 0:8], cand[:, h, :])
                    then_top(ins)
                    for h in range(HEADS):
                        V.max_index(best_i[:, h, 0:8], best_v[:, h, 0:8], cand[:, h, :])
                        ins = V.match_replace(cand2[:, h, :], best_v[:, h, 0:8], cand[:, h, :], LOWEST)
                    then_top(ins)
                    for h in range(HEADS):
                        ins = V.max(best_v[:, h, 8:16], cand2[:, h, :])
                    then_top(ins)
                    for h in range(HEADS):
                        ins = V.max_index(best_i[:, h, 8:16], best_v[:, h, 8:16], cand2[:, h, :])
                    then_top(ins)
                    chained(V.tensor_copy(best_f[:], best_i[:]))
                    chained(V.tensor_copy(gate_z[:], best_v[:, :, 0:1].rearrange("p h o -> p (h o)")))
                    V.tensor_tensor(best_v[:], best_v[:], gate_z[:].unsqueeze(2).to_broadcast([P, HEADS, TOPK]),
                                    ALU.subtract).then_inc(S["exp_in"], 1)
                    for h in range(HEADS):
                        V.tensor_tensor(pick[:], best_f[:, h, :].unsqueeze(2).to_broadcast([P, TOPK, NCAND]),
                                        iota_f[:, 0:NCAND].unsqueeze(1).to_broadcast([P, TOPK, NCAND]),
                                        ALU.is_equal).then_inc(S["topk"], 1)
                        dve.wait_ge(S["topk"], b * 24 + (l * TB * 24 + 3 * h + 1))
                        V.tensor_tensor(pick[:], pick[:], code[:, h, :].unsqueeze(1).to_broadcast([P, TOPK, NCAND]),
                                        ALU.mult).then_inc(S["topk"], 1)
                        dve.wait_ge(S["topk"], b * 24 + (l * TB * 24 + 3 * h + 2))
                        V.tensor_reduce(best_e[:, h, :], pick[:], AX_X, ALU.add).then_inc(S["topk"], 1)
                        dve.wait_ge(S["topk"], b * 24 + (l * TB * 24 + 3 * h + 3))
                    chained(V.tensor_copy(expert[:], best_e[:].rearrange("p h k -> p (h k)")))
                    V.tensor_scalar(expert_i[:], expert[:], 7, None, ALU.logical_shift_right)
                    chained(V.tensor_scalar(expert_j[:], expert[:], NK - 1, None, ALU.bitwise_and))
                    V.tensor_copy(i_f[:], expert_i[:])
                    chained(V.tensor_copy(j_f[:], expert_j[:]))
                    dve.wait_ge(S["exp_out"], b + (l * TB + 1))
                    chained(V.tensor_reduce(gate_z[:], gate[:], AX_X, ALU.add))
                    chained(V.reciprocal(gate_z[:], gate_z[:]))
                    V.tensor_tensor(gate[:], gate[:], gate_z[:].unsqueeze(2).to_broadcast([P, HEADS, TOPK]),
                                    ALU.mult).then_inc(S["tr_read"], 1)
                    dve.wait_ge(S["tr_mm"], b + (l * TB + 1))
                    V.tensor_copy(i_t[:, bass.ds(b * P, P)], ps[4][:, 0:P])
                    V.tensor_copy(j_t[:, bass.ds(b * P, P)], ps[4][:, P:2 * P])
                    chained(V.tensor_copy(gate_t[:, 2, bass.ds(b * P, P)], ps[4][:, 2 * P:3 * P]))
                    assert chain[0] - base == LINKS, chain[0] - base
                chain[0] = base + TB * LINKS
                for part_no in range(2):
                    link(V.tensor_copy(gate_bf[:], gate_t[:, 2, :]))
                    link(V.tensor_copy(gate_t[:, part_no, :], gate_bf[:]))
                    link(V.tensor_tensor(gate_t[:, 2, :], gate_t[:, 2, :], gate_t[:, part_no, :], ALU.subtract))
                groups = l * T // GROUP

                def one_hots(r, s, head):
                    if not head:
                        dve.wait_ge(S["g_mm"], r * 4 + (2 * (groups + s) - 2))
                    for n in range(GROUP):
                        t = bass.ds(r * (2 * GROUP) + (s * GROUP + n), 1)
                        V.tensor_scalar(oh_i[:, s, n, :], iota_bf[:], i_t[:, t], None, ALU.is_equal)
                        for w in range(3):
                            ins = V.tensor_scalar(oh_j[:, s, n, w, :], iota_bf[:], j_t[:, t], gate_t[:, w, t],
                                                  ALU.is_equal, ALU.mult)
                    ins.then_inc(S["oh_ready"], 1)

                for s in range(2):
                    one_hots(0, s, l == 0)
                with dve.Fori(1, T // GROUP // 2) as r:
                    for s in range(2):
                        one_hots(r, s, False)

                first = BASE[f"v{l}"]

                def gated(grp, s, head=False):
                    grp, s = grp + s // RING, s % RING
                    dve.wait_ge(act_ld[s], grp * 16 + (l * EXPERT_TILES // RING + 1) * 16)
                    dve.wait_ge(g_ld[s], grp * 16 + (l * EXPERT_TILES // RING + 1) * 16)
                    if not head:
                        dve.wait_ge(S["pl_ready"], grp * RING + (l * EXPERT_TILES + s - 1))
                    V.tensor_tensor(prod[:, s % 2, :], act_ring[:, s, :], g_ring[:, s, :], ALU.mult
                                    ).then_inc(S["p_ready"], 1)

                def prod_lo(grp, s):
                    dve.wait_ge(S["ph_ready"], grp * RING + (l * EXPERT_TILES + s + 1))
                    V.tensor_tensor(h_lo[:, s % 2, :], prod[:, s % 2, :], h_hi[:, s % 2, :].bitcast(F32),
                                    ALU.subtract).then_inc(S["pl_ready"], 1)

                gated(0, 0, True)
                gated(0, 1, True)
                last = EXPERT_TILES // RING - 1

                def products(i):
                    for s in range(RING):
                        prod_lo(i, s)
                        gated(i, s + 2)

                rounds = 0
                if l == 0:
                    rounds = MOD_C_ROUNDS
                    with dve.Fori(0, rounds) as i:
                        products(i)
                        for s in range(2):
                            dve.wait_ge(mod_c_ld[s], i * 16 + 16)
                            mod_row_sum(mod_c_ring[:, s, :], mod[:, bass.ds(i * 2 + (MOD - MOD_C + s), 1)]
                                        ).then_inc(S["mod_c_done"], 1)
                with dve.Fori(rounds, last) as i:
                    products(i)
                for s in range(RING):
                    prod_lo(last, s)
                    if s < 2:
                        gated(last, s + 2)
                dve.wait_ge(S["tile_done"], first + EXPERT_TILES)
                for k in range(KC):
                    ins = V.scalar_tensor_tensor(out=x[:, k, :], in0=out_bank(k), scalar=modc(l, 5, k), in1=x[:, k, :],
                                                 op0=ALU.mult, op1=ALU.add)
                    ins.then_inc(S["x_ready"], 1)

            def mod_row_sum(w, dst):
                return V.scalar_tensor_tensor(out=w, in0=w, scalar=1.0, in1=c_row[:], op0=ALU.mult, op1=ALU.mult,
                                              accum_out=dst)

            def add_bias(at, n, src):
                link(V.tensor_tensor(mod[:, at:at + n], src, cols[:, COLS["mod_b"] + at:COLS["mod_b"] + at + n],
                                     ALU.add))

            def norm_gain(n):
                l, which = n // 2, n % 2
                at = l * 6 * KC + (1 + 3 * which) * KC
                name = COLS[("norm1_g", "norm2_g")[which]] + l * KC
                return V.scalar_tensor_tensor(out=gain[:, n, :], in0=mod[:, at:at + KC], scalar=1.0,
                                              in1=cols[:, name:name + KC], op0=ALU.add, op1=ALU.mult)

            dve.wait_ge(S["c_ready"], 1)
            with dve.Fori(0, MOD_A // RING) as i:
                for s in range(RING):
                    dve.wait_ge(ld[s], i * 16 + 16)
                    mod_row_sum(w_raw[:, s, :], mod[:, bass.ds(i * RING + s, 1)]).then_inc(S["mod_a_done"], 1)
            dve.wait_ge(S["mod_a_done"], MOD_A)
            dve.wait_ge(S["consts"], 1)
            V.tensor_copy(iota_bf[:], iota_i[:])
            V.tensor_copy(iota_f[:], iota_i[:])
            add_bias(0, MOD_A, mod[:, 0:MOD_A])
            norm_gain(0).then_inc(S["mod_ready"], 1)
            dve.wait_ge(S["mod_ready"], 1)

            norm_dve(0, lambda k: gain[:, 0, k:k + 1], lambda k: modc(0, 0, k))
            dve.wait_ge(S["hl_ready"], KC)
            link(V.memset(a_pad[:, :, 0:PAD], 0.0))

            def convolve(c):
                dve.wait_ge(S["evac"], 2 * c + 2)
                V.tensor_tensor(a_pad[:, c, PAD:PAD + T], z[:, 2 * (c % 2), :], z[:, 2 * (c % 2) + 1, :], ALU.mult
                                ).then_inc(S["glu_done"], 1)
                dve.wait_ge(S["glu_done"], c + 1)
                link(V.tensor_scalar(conv[:, c, :], a_pad[:, c, 0:T], col("conv_w", c * TAPS), col("conv_b", c),
                                     ALU.mult, ALU.add))
                before = chain[0]
                with dve.Fori(1, TAPS) as tap:
                    V.scalar_tensor_tensor(out=conv[:, c, :], in0=a_pad[:, c, bass.ds(tap, T)],
                                           scalar=cols[:, bass.ds(tap + (COLS["conv_w"] + c * TAPS), 1)],
                                           in1=conv[:, c, :], op0=ALU.mult, op1=ALU.add
                                           ).then_inc(S["dve_chain"], 1)
                    dve.wait_ge(S["dve_chain"], tap + before)
                chain[0] = before + TAPS - 1

            for c in range(AC - 1):
                convolve(c)
            ln_centre(0, v_c)
            convolve(AC - 1)
            ln_scale(0, v_c, "gln_g")
            ln_centre(1, conv)
            dve.wait_ge(S["mod_b_done"], MOD_B)
            add_bias(MOD_A, MOD_B, ps[5][:, 0:MOD_B])
            norm_gain(1).then_inc(S["mod_ready"], 1)
            ln_scale(1, conv, "cln_g")
            for c in range(AC):
                dve.wait_ge(S["mixed"], c + 1)
                V.tensor_tensor(z[:, c % 2, :].rearrange("p (n t) -> p n t", t=P),
                                ps[6 + c % 2][:].rearrange("p (n t) -> p n t", t=P),
                                bs[:, c:c + 1, :].to_broadcast([P, T // P, P]), ALU.add).then_inc(S["mixed_read"], 1)
                dve.wait_ge(S["mixed_read"], c + 1)
                V.tensor_tensor(u_c[:, c, :], u_c[:, c, :], z[:, c % 2, :], ALU.mult).then_inc(S["bout"], 1)
            for c in range(KC):
                dve.wait_ge(S["hh_ready"], KC + c + 1)
                src = conv[:, c, :] if c < AC else u_c[:, c - AC, :]
                V.tensor_tensor(h_lo[:, c, :], src, h_hi[:, c, :].bitcast(F32), ALU.subtract
                                ).then_inc(S["hl_ready"], 1)
            residual_dve("ev_out")
            norm_dve(1, lambda k: gain[:, 1, k:k + 1], lambda k: modc(0, 3, k))
            peer_dve(0)

            dve.wait_ge(S["mod_c_done"], MOD_C)
            add_bias(MOD_A + MOD_B, MOD_C, mod[:, MOD_A + MOD_B:MOD])
            norm_gain(2)
            norm_gain(3).then_inc(S["mod_ready"], 1)
            dve.wait_ge(S["mod_ready"], 3)
            norm_dve(2, lambda k: gain[:, 2, k:k + 1], lambda k: modc(1, 0, k))
            dve.wait_ge(S["hl_ready"], HR[2] + KC)
            link(V.memset(m_pad[:, :, 0:2], 0.0))
            for c in range(KC):
                m = c % 2
                dve.wait_ge(S["evac"], EVAC["od_in"] + 3 * c + 3)
                link(V.tensor_tensor(m_pad[:, m, 2:2 + T], zc[:, 0, :], zc[:, 1, :], ALU.mult))
                link(V.tensor_scalar(y_c[:, c, :], m_pad[:, m, 0:T], col("od_conv_w", 3 * c), None, ALU.mult))
                for k in (1, 2):
                    link(V.scalar_tensor_tensor(out=y_c[:, c, :], in0=m_pad[:, m, k:k + T],
                                                scalar=col("od_conv_w", 3 * c + k), in1=y_c[:, c, :],
                                                op0=ALU.mult, op1=ALU.add))
                V.tensor_tensor(y_c[:, c, :], y_c[:, c, :], zc[:, 2, :], ALU.mult).then_inc(S["z_free"], 1)
            dve.wait_ge(S["z_free"], KC)
            for c in range(KC):
                dve.wait_ge(S["hh_ready"], 3 * KC + KC + c + 1)
                V.tensor_tensor(h_lo[:, c, :], y_c[:, c, :], h_hi[:, c, :].bitcast(F32), ALU.subtract
                                ).then_inc(S["hl_ready"], 1)
            residual_dve("od_out")
            norm_dve(3, lambda k: gain[:, 3, k:k + 1], lambda k: modc(1, 3, k))
            peer_dve(1)
            norm_dve(4, lambda k: col("final_g", k), None)

        @block.tensor
        def _(pe):
            MM = nc.tensor.matmul

            def operands_ready(grp, s):
                pe.wait_ge(S["hi_ready"], grp * RING + s + 1)
                pe.wait_ge(S["lo_ready"], grp * RING + s + 1)

            def project(grp, s, banked, operand=None):
                operands_ready(grp, s)
                if banked is not None:
                    pe.wait_ge(S["evac"], banked - 1)
                o = ps[s % 2][:]
                for k in range(KC):
                    hi = w_hi[:, s % 2, k * P:(k + 1) * P]
                    lo = w_lo[:, s % 2, k * P:(k + 1) * P]
                    if operand is not None:
                        pe.wait_ge(S["hh_ready"], operand * KC + k + 1)
                    MM(o, hi, h_hi[:, k, :], start=(k == 0), stop=False)
                    MM(o, lo, h_hi[:, k, :], start=False, stop=False)
                    if operand is not None:
                        pe.wait_ge(S["hl_ready"], operand * KC + k + 1)
                    ins = MM(o, hi, h_lo[:, k, :], start=False, stop=(k == KC - 1))
                ins.then_inc(S["tile_done"], 1)

            def projections(name, n, operand):
                g, b = BASE[name] // RING, EVAC[name]
                for s in range(RING):
                    project(g, s, None if b + s < 2 else b + s, operand if s == 0 else None)
                with pe.Fori(1, n // RING) as i:
                    for s in range(RING):
                        project(i + g, s, i * RING + (b + s))

            def projections_and_squares(name, operand, n):
                g, b = BASE[name] // RING, EVAC[name]
                for k in range(KC + 2):
                    if k < KC:
                        project(g + k // RING, k % RING, b + k, operand if k == 0 else None)
                    if k >= 2:
                        square_sum(n, k - 2)

            def square_sum(n, k):
                pe.wait_ge(S["sq_ready"], n * KC + k + 1)
                ins = MM(ps[5][:], ones[:], sq[:, k, :], start=(k == 0), stop=(k == KC - 1))
                if k == KC - 1:
                    ins.then_inc(S["ssum"], 1)

            def sum_squares(n):
                for k in range(KC):
                    square_sum(n, k)

            def ln_sum(src):
                for c in range(AC):
                    ins = MM(ps[4][:], ones[:], src[:, c, :], start=(c == 0), stop=(c == AC - 1))
                ins.then_inc(S["ln_mm"], 1)

            def peer_pe(l):
                projections(f"q{l}", Q_TILES, 2 + 3 * l)
                pe.wait_ge(S["evac"], EVAC[f"u{l}"])
                for grp in range(TB * 4):
                    b = grp // 4
                    if grp >= 2:
                        pe.wait_ge(S["sc_ev"], l * TB * 4 + grp - 1)
                    for w in range(4):
                        hp = 4 * (grp % 4) + w
                        ins = MM(ps[2 + grp % 2][:, w * NK:(w + 1) * NK], q[:, hp, b * P:(b + 1) * P],
                                 sk[:, l, hp % 2, :], start=True, stop=True)
                    ins.then_inc(S["sc_mm"], 1)
                first, banked = BASE[f"u{l}"] // RING, EVAC[f"u{l}"]
                per = TILES_PER_BLOCK // RING
                with pe.Fori(0, TB) as b:
                    with pe.Fori(0, per) as r:
                        for s in range(RING):
                            project(b * per + r + first, s, b * TILES_PER_BLOCK + r * RING + (banked + s))
                    pe.wait_ge(S["tr_read"], b + (l * TB + 1))
                    nc.tensor.transpose(ps[4][:, 0:P], i_f[:], ident[:])
                    nc.tensor.transpose(ps[4][:, P:2 * P], j_f[:], ident[:])
                    nc.tensor.transpose(ps[4][:, 2 * P:3 * P], gate[:].rearrange("p h k -> p (h k)"), ident[:]
                                        ).then_inc(S["tr_mm"], 1)
                at = TB * per
                groups = l * T // GROUP
                with pe.Fori(0, T // GROUP // RING) as r:
                    for s in range(RING):
                        project(r + (at + first), s, r * RING + (banked + at * RING + s))
                        pe.wait_ge(S["oh_ready"], r * RING + (groups + s + 1))
                        for w in range(2):
                            pe.wait_ge(S["g_ev"], r * 8 + (2 * groups + 2 * s + w + 1))
                            for n in range(4):
                                for p3 in range(3):
                                    ins = MM(ps[2 + w][:, n * NK:(n + 1) * NK], oh_i[:, s % 2, 4 * w + n, :],
                                             oh_j[:, s % 2, 4 * w + n, p3, :], start=(p3 == 0), stop=(p3 == 2))
                            ins.then_inc(S["g_mm"], 1)
                at += T // GROUP // RING
                with pe.Fori(0, EXPERT_TILES // RING - at) as i:
                    for s in range(RING):
                        project(i + (at + first), s, i * RING + (banked + at * RING + s))
                first = BASE[f"v{l}"] // RING
                pe.wait_ge(S["g_ev"], (l + 1) * 2 * T // GROUP + 2)
                pe.wait_ge(S["evac"], banked + EXPERT_TILES - 1)

                def accumulate(grp, s, start, stop):
                    operands_ready(grp + first, s)
                    pe.wait_ge(S["ph_ready"], grp * RING + (l * EXPERT_TILES + s + 1))
                    pe.wait_ge(S["pl_ready"], grp * RING + (l * EXPERT_TILES + s + 1))
                    for k in range(KC):
                        hi = w_hi[:, s % 2, k * P:(k + 1) * P]
                        lo = w_lo[:, s % 2, k * P:(k + 1) * P]
                        if start and k == 4:
                            pe.wait_ge(S["evac"], banked + EXPERT_TILES)
                        MM(out_bank(k), hi, h_hi[:, s % 2, :], start=start, stop=False)
                        MM(out_bank(k), hi, h_lo[:, s % 2, :], start=False, stop=False)
                        ins = MM(out_bank(k), lo, h_hi[:, s % 2, :], start=False, stop=stop)
                    ins.then_inc(S["tile_done"], 1)

                last = EXPERT_TILES // RING - 1
                for s in range(RING):
                    accumulate(0, s, s == 0, False)
                with pe.Fori(1, last) as i:
                    for s in range(RING):
                        accumulate(i, s, False, False)
                for s in range(RING):
                    accumulate(last, s, False, s == RING - 1)

            pe.wait_ge(S["inputs"], 16 * N_INPUTS)
            pe.wait_ge(S["consts"], 1)
            sum_squares(0)
            projections("ev_in", EV_IN, 0)
            pe.wait_ge(S["evac"], EV_IN)
            ln_sum(v_c)
            pe.wait_ge(S["ln_sqd"], 1)
            ln_sum(ln_sq)
            pe.wait_ge(S["c_ready"], 2)
            for m in range(MOD_B):
                s = m % MOD_B_RING
                pe.wait_ge(mod_b_ld[s], 16 * (m // MOD_B_RING + 1))
                for k in range(KC):
                    ins = MM(ps[5][:, m:m + 1], mod_b_ring[:, s, k * P:(k + 1) * P], c_act[:, k:k + 1],
                             start=(k == 0), stop=(k == KC - 1))
                ins.then_inc(S["mod_b_done"], 1)
            for c in range(AC):
                pe.wait_ge(S["ln_out"], c + 1)
                if c >= 2:
                    pe.wait_ge(S["v_tok_ready"], c - 1)
                for n in range(T // P):
                    ins = nc.tensor.transpose(ps[2 + c % 2][:, n * P:(n + 1) * P], v_c[:, c, n * P:(n + 1) * P],
                                              ident[:])
                ins.then_inc(S["v_tr"], 1)
            ln_sum(conv)
            for c in range(AC):
                pe.wait_ge(S["v_tok_ready"], c + 1)
                if c >= 2:
                    pe.wait_ge(S["mixed_read"], c - 1)
                for n in range(T // P):
                    ins = MM(ps[6 + c % 2][:, n * P:(n + 1) * P], v_tok[:, c, n * P:(n + 1) * P], ws[:, c, :],
                             start=True, stop=True)
                ins.then_inc(S["mixed"], 1)
                if c == 1:
                    pe.wait_ge(S["ln_sqd"], 2)
                    ln_sum(ln_sq)
            projections_and_squares("ev_out", 1, 1)
            peer_pe(0)
            sum_squares(2)
            projections("od_in", OD_IN, 3)
            projections_and_squares("od_out", 4, 3)
            peer_pe(1)
            sum_squares(4)


N_INPUTS = 5
RESIDUAL = (1, 3)
XR = [0, KC, 2 * KC, 3 * KC, 4 * KC]
HR = [0, 2 * KC, 3 * KC, 5 * KC, 6 * KC]


def kernel(**inputs):
    import concourse.bacc as bacc
    from concourse.bass_utils import run_bass_kernel_spmd

    a = {n: np.asarray(v) for n, v in inputs.items()}

    def tiles(w, order=None):
        t = w.reshape(KC, P, -1, P).transpose(2, 1, 0, 3)
        return t if order is None else t[order]

    ev_order = [i for c in range(AC) for i in (c, AC + c)] + [3 * AC + c for c in range(AC)] \
        + [2 * AC + c for c in range(AC)]
    od_order = [i for c in range(KC) for i in (KC + c, 2 * KC + c, c)]
    parts = []
    for l in range(2):
        if l == 0:
            parts += [tiles(a["ev_w_in"][0], ev_order), tiles(a["ev_w_out"][0])]
        else:
            parts += [tiles(a["od_w_in"][0], od_order), tiles(a["od_w_out"][0])]
        parts.append(tiles(a["pk_wq"][l]))
        parts.append(a["pk_u"][l].reshape(NK, NK, KC, P).transpose(1, 3, 2, 0))
        parts.append(a["pk_v"][l].reshape(NK, NK, D).transpose(1, 0, 2).reshape(NK, P, KC, P))
    stream = np.empty((TILES, P, D), a["x"].dtype)
    at = 0
    for p in parts:
        stream[at:at + len(p)].reshape(len(p), P, KC, P)[:] = p
        at += len(p)
    assert at == TILES
    rows = a["mod_w"].transpose(0, 2, 1).reshape(MOD, P, D)
    mod_rows = np.concatenate([rows[:MOD_A], rows[MOD - MOD_C:]])
    mod_cols = tiles(a["mod_w"][0])[MOD_A:MOD_A + MOD_B].reshape(MOD_B, P, D)

    def columns(v):
        return v.reshape(-1, P).T

    cols = np.concatenate([
        columns(a["c"]), columns(a["mod_b"]), columns(a["norm1_g"]), columns(a["norm2_g"]),
        a["ev_conv_w"][0].reshape(TAPS, AC, P).transpose(2, 1, 0).reshape(P, AC * TAPS),
        columns(a["ev_conv_b"]), columns(a["ev_cln_g"]), columns(a["ev_cln_b"]), columns(a["ev_gln_g"]),
        columns(a["ev_gln_b"]), a["od_conv_w"][0].reshape(3, KC, P).transpose(2, 1, 0).reshape(P, 3 * KC),
        columns(a["final_g"])], axis=1)
    arrays = {
        "stream": stream,
        "mod_rows": mod_rows,
        "mod_cols": mod_cols,
        "c_in": np.broadcast_to(a["c"], (P, D)),
        "x_in": a["x"][0].T.reshape(KC, P, T).transpose(1, 0, 2),
        "cols_in": cols,
        "sk_in": a["pk_subkeys"].transpose(3, 0, 1, 2),
        "ws_in": a["ev_ws"][0].transpose(2, 0, 1),
        "bs_in": np.broadcast_to(a["ev_bs"][0][None], (P, AC, P)),
    }
    arrays = {n: np.ascontiguousarray(v) for n, v in arrays.items()}
    nc = bacc.Bacc("TRN2", target_bir_lowering=False, num_devices=1)
    args = {n: nc.dram_tensor(n, v.shape, mybir.dt.from_np(v.dtype), kind="ExternalInput").ap()
            for n, v in arrays.items()}
    out = nc.dram_tensor("out", [P, KC, T], F32, kind="ExternalOutput").ap()
    act_dram = nc.dram_tensor("act_dram", [EXPERT_TILES, P, T], F32).ap()
    gate_dram = nc.dram_tensor("gate_dram", [T // HALF, P, NK, HALF], F32).ap()
    build(nc, out=out, act_dram=act_dram, gate_dram=gate_dram, **args)
    r = run_bass_kernel_spmd(nc, [arrays], core_ids=[0])
    got = r.results[0]["out"]
    return np.ascontiguousarray(got.transpose(2, 1, 0).reshape(1, T, D))
```

```python
from contextlib import ExitStack

import numpy as np

import concourse.bass as bass
from concourse import mybir

F32 = mybir.dt.float32
F32R = mybir.dt.float32r
BF16 = mybir.dt.bfloat16
U32 = mybir.dt.uint32
I32 = mybir.dt.int32
ALU = mybir.AluOpType
ACT = mybir.ActivationFunctionType
AX_X = mybir.AxisListType.X

P = 128
D = 1024
KC = D // P
T = 512
EPS = 1e-6
AC = 512 // P
TAPS = 31
HEADS = 8
TOPK = 16
NK = 128
TB = T // P
LOWEST = -3.0e38

MOD = 2 * 6 * KC
MOD_A = 2 * KC
MOD_G = KC
MOD_B = MOD_G + 2 * KC
MOD_C = MOD - MOD_A - MOD_B
MOD_A_RING = 12
MOD_B_RING = 4
MOD_G_LAG = 5
MOD_C_ROUNDS = MOD_C // 2
EV_IN, EV_OUT, OD_IN, OD_OUT = 16, KC, 3 * KC, KC
Q_TILES, EXPERT_TILES = 2 * HEADS, NK
BASE = {}
EVAC = {}
_g = _b = 0
for _name, _n, _banked in [("ev_in", EV_IN, 1), ("ev_out", EV_OUT, 1), ("q0", Q_TILES, 1), ("u0", EXPERT_TILES, 1),
                           ("v0", EXPERT_TILES, 0), ("od_in", OD_IN, 1), ("od_out", OD_OUT, 1), ("q1", Q_TILES, 1),
                           ("u1", EXPERT_TILES, 1), ("v1", EXPERT_TILES, 0)]:
    BASE[_name], EVAC[_name] = _g, _b
    _g += _n
    _b += _n * _banked
TILES = _g
RING = 4
assert all(b % RING == 0 for b in BASE.values())

PAIRS = [BASE[n] for n in ("ev_in", "ev_out", "q0", "od_in", "od_out", "q1")]

TILES_PER_BLOCK = 12
GROUP = 8
HALF = 64

ROWS = [(a, TOPK // (a + 1)) for a in range(TOPK // 2)]
OFFS = np.cumsum([0] + [n for _, n in ROWS]).tolist()
NCAND = OFFS[-1] + TOPK // 2

COLS = {}
_c = 0
for _name, _n in [("mod_b", MOD), ("norm1_g", 2 * KC), ("norm2_g", 2 * KC), ("conv_w", AC * TAPS),
                  ("conv_b", AC), ("cln_g", AC), ("cln_b", AC), ("gln_g", AC), ("gln_b", AC),
                  ("od_conv_w", 3 * KC), ("final_g", KC)]:
    COLS[_name] = _c
    _c += _n
NCOLS = _c


def build(nc, stream, mod_rows, x_in, c_in, cols_in, sk_in, ws_in, bs_in, out, act_dram, gate_dram):
    with ExitStack() as ctx:
        def sb(name, shape, dt=F32):
            return ctx.enter_context(nc.sbuf_tensor(name, shape, dt))

        def sem(name):
            return ctx.enter_context(nc.semaphore(name))

        ps = [ctx.enter_context(nc.psum_tensor(f"bank{i}", [P, 512], F32)) for i in range(8)]

        x = sb("x", [P, KC, T])
        h_hi = sb("h_hi", [P, KC, T], F32R)
        h_lo = sb("h_lo", [P, KC, T], F32R)
        w_raw = sb("w_raw", [P, RING, D])
        w_hi = sb("w_hi", [P, 2, D], F32R)
        w_lo = sb("w_lo", [P, 2, D], F32R)
        shared = sb("shared", [P, 16384])
        oh_i = sb("oh_i", [P, 2, GROUP, NK], BF16)
        oh_j = sb("oh_j", [P, 2, GROUP, 3, NK], BF16)
        act_ring = sb("act_ring", [P, RING, T])
        i_t = sb("i_t", [P, T])
        j_t = sb("j_t", [P, T])
        gate_t = sb("gate_t", [P, 3, T])
        w_hi_first = sb("w_hi_first", [P, D], F32R)
        w_lo_first = sb("w_lo_first", [P, D], F32R)
        gate_bf = sb("gate_bf", [P, T], BF16)
        oh_words = oh_j[:].rearrange("p a b c d -> p (a b c d)").bitcast(F32)
        used = [0]

        def topk_part(a, b):
            at = used[0]
            used[0] += a * b
            return oh_words[:, at:at + a * b].rearrange("p (a b) -> p a b", a=a)

        top_v = topk_part(2 * HEADS, TOPK)
        top_i = topk_part(2 * HEADS, TOPK).bitcast(U32)
        top_f = topk_part(2 * HEADS, TOPK)
        cand = topk_part(HEADS, NCAND)
        code = topk_part(HEADS, NCAND)
        best_v = topk_part(HEADS, TOPK)
        best_i = topk_part(HEADS, TOPK).bitcast(U32)
        best_f = topk_part(HEADS, TOPK)
        best_e = topk_part(HEADS, TOPK)
        cand2 = sb("cand2", [P, HEADS, NCAND])
        expert = sb("expert", [P, HEADS * TOPK], I32)
        expert_i = sb("expert_i", [P, HEADS * TOPK], I32)
        expert_j = sb("expert_j", [P, HEADS * TOPK], I32)
        i_f = sb("i_f", [P, HEADS * TOPK])
        j_f = sb("j_f", [P, HEADS * TOPK])
        gate = sb("gate", [P, HEADS, TOPK])
        gate_z = sb("gate_z", [P, HEADS])
        cols = sb("cols", [P, NCOLS])
        c_row = sb("c_row", [P, D])
        mod = sb("mod", [P, MOD])
        gain = sb("gain", [P, 4, KC])
        sk = sb("sk", [P, 2, 2, NK])
        ws = sb("ws", [P, AC, P])
        bs = sb("bs", [P, AC, P])
        ones = sb("ones", [P, P])
        ident = sb("ident", [P, P])
        iota_i = sb("iota_i", [P, P], I32)
        iota_bf = sb("iota_bf", [P, P], BF16)
        iota_f = sb("iota_f", [P, P])
        var_c = sb("var_c", [P, 2 * TB])
        root_c = sb("root_c", [P, 2 * TB])
        root_t = sb("root_t", [P, 2 * TB])

        def part(at, *dims):
            n = int(np.prod(dims))
            v = shared[:, at:at + n]
            if len(dims) == 2:
                return v.rearrange("p (a b) -> p a b", a=dims[0])
            if len(dims) == 3:
                return v.rearrange("p (a b c) -> p a b c", a=dims[0], b=dims[1])
            return v

        sq = part(0, KC, T)
        mod_a_ring = part(KC * T, MOD_A_RING, D)
        PAD = TAPS - 1
        z = part(0, 4, T)
        a_pad = part(2048, AC, T + PAD + 2)
        conv = part(4224, AC, T)
        odd_taps = part(10368, 1, T)
        v_c = part(6272, AC, T)
        u_c = part(8320, AC, T)
        v_tok = part(10368, AC, T)
        z_more = part(12416, 4, T)
        ln_sq = [z, part(2048, AC, T)]
        ln_bank = [4, 5]
        zc = part(0, 4, T)
        m_pad = part(2048, 2, T + 4)
        y_c = part(4096, KC, T)
        y_slot = part(12416, 2, T)
        q = part(0, Q_TILES, T)
        work = part(0, 2 * HEADS, NK)
        work2 = part(2048, 2 * HEADS, NK)
        pick = part(4096, TOPK, NCAND)
        scores = part(8192, TB, 2 * HEADS, NK)
        gate_st = part(0, 2, NK, HALF)
        g_ring = part(0, RING, T)
        prod = part(2048, 2, T)
        mod_c_ring = part(4096, 2, D)
        mod_b_ring = [oh_words[:, i * D:(i + 1) * D] for i in range(3)]
        mod_b_ring.append(oh_i[:].rearrange("p a b c -> p (a b c)").bitcast(F32))
        stat = act_ring

        ld = [sem(f"ld{i}") for i in range(RING)]
        act_st = [sem(f"act_st{i}") for i in range(RING)]
        act_ld = [sem(f"act_ld{i}") for i in range(RING)]
        g_ld = [sem(f"g_ld{i}") for i in range(RING)]
        mod_a_ld = [sem(f"mod_a_ld{i}") for i in range(MOD_A_RING)]
        mod_b_ld = [sem(f"mod_b_ld{i}") for i in range(MOD_B_RING)]
        mod_c_ld = [sem(f"mod_c_ld{i}") for i in range(2)]
        g_st = [sem(f"g_st{i}") for i in range(2)]
        names = ("inputs late_inputs c_in consts ws_ready mod_a_done mod_g_prod mod_b_done mod_c_done "
                 "c_ready mod_ready hi_ready lo_ready tile_done bank_done evac hh_ready hl_ready x_ready "
                 "sq_ready ssum diag_ready inv_ready t_ready glu_done act_chain dve_chain pool_chain tap "
                 "conv_done ln_mm ln_sqd centred scaled ln_out v_tr v_tok_ready mixed mixed_read bout "
                 "top_step out_ready stored sc_mm sc_ev topk exp_in exp_out tr_mm tr_read oh_ready g_mm "
                 "g_ev p_ready ph_ready pl_ready z_free").split()
        S = {n: sem(n) for n in names}

        def col(name, i):
            return cols[:, COLS[name] + i:COLS[name] + i + 1]

        def modc(l, which, k):
            i = l * 6 * KC + which * KC + k
            return mod[:, i:i + 1]

        def glu_in(c, which):
            return (z, z_more)[c // 2][:, 2 * (c % 2) + which, :]

        def out_bank(k):
            return ps[(k + 5) % 8][:]

        def first_of_phase(grp, s):
            return isinstance(grp, int) and grp * RING + s in PAIRS

        def hi_of(grp, s):
            return w_hi_first[:] if first_of_phase(grp, s) else w_hi[:, s % 2, :]

        def lo_of(grp, s):
            return w_lo_first[:] if first_of_phase(grp, s) else w_lo[:, s % 2, :]

        block = ctx.enter_context(nc.Block())

        @block.sync
        def _(sp):
            sp.dma_start(c_row[:], c_in).then_inc(S["c_in"], 16)
            sp.dma_start(x[:], x_in).then_inc(S["inputs"], 16)
            for i in range(MOD_A):
                if i >= MOD_A_RING:
                    sp.wait_ge(S["mod_a_done"], i - MOD_A_RING + 1)
                sp.dma_start(mod_a_ring[:, i % MOD_A_RING, :], mod_rows[MOD_A_ORDER[i]]
                             ).then_inc(mod_a_ld[i % MOD_A_RING], 16)

            def load(grp, s):
                sp.wait_ge(S["hi_ready"], grp * RING + s - RING + 1)
                sp.wait_ge(S["lo_ready"], grp * RING + s - RING + 1)
                sp.dma_start(w_raw[:, s, :], stream[grp * RING + s]).then_inc(ld[s], 16)

            for s in range(RING):
                sp.dma_start(w_raw[:, s, :], stream[s]).then_inc(ld[s], 16)
            sp.dma_start(sk[:], sk_in).then_inc(S["late_inputs"], 16)
            sp.dma_start(ws[:], ws_in).then_inc(S["late_inputs"], 16)
            sp.dma_start(bs[:], bs_in).then_inc(S["late_inputs"], 16)

            def load_mod_b(m):
                s = m % MOD_B_RING
                if m >= MOD_B_RING:
                    sp.wait_ge(S["mod_b_done"], m - MOD_B_RING + 1)
                sp.dma_start(mod_b_ring[s], mod_rows[MOD_A + m]).then_inc(mod_b_ld[s], 16)

            for m in range(MOD_B_RING):
                load_mod_b(m)
            at = BASE["ev_out"] // RING + 1
            for g in range(RING, at * RING):
                load(g // RING, g % RING)
                m = g - MOD_G_LAG - 2
                if MOD_B_RING <= m < MOD_G + MOD_B_RING:
                    load_mod_b(m)
            for k in range(KC):
                load(at + k // RING, k % RING)
                for m in range(MOD_G + MOD_B_RING + 2 * k, MOD_G + MOD_B_RING + 2 * k + 2):
                    if m < MOD_B:
                        load_mod_b(m)
            at += KC // RING

            for l in range(2):
                first = BASE[f"v{l}"] // RING
                with sp.Fori(at, first) as i:
                    for s in range(RING):
                        load(i, s)

                def load_products(j4, s):
                    sp.dma_start(act_ring[:, s, :], act_dram[j4 * RING + s]).then_inc(act_ld[s], 16)
                    sp.dma_start(g_ring[:, s, :].rearrange("p (b t) -> p b t", t=HALF),
                                 gate_dram[:, :, j4 * RING + s, :].rearrange("b p t -> p b t")
                                 ).then_inc(g_ld[s], 16)

                for s in range(2):
                    load(first, s)
                for r in range(2):
                    sp.wait_ge(g_st[r], 16 * ((l + 1) * T // HALF // 2 + 1))
                for s in range(RING):
                    sp.wait_ge(act_st[s], 16 * (l + 1) * EXPERT_TILES // RING)
                    load_products(0, s)
                    if s < 2:
                        load(first, s + 2)

                def expert_loads(i):
                    for s in range(RING):
                        load(i + first, s)
                        sp.wait_ge(S["p_ready"], i * RING + (l * EXPERT_TILES + s - RING + 1))
                        load_products(i, s)

                rounds = 0
                if l == 0:
                    rounds = MOD_C_ROUNDS
                    for s in range(2):
                        sp.dma_start(mod_c_ring[:, s, :], mod_rows[MOD_A + MOD_B + s]).then_inc(mod_c_ld[s], 16)
                    with sp.Fori(1, rounds) as i:
                        expert_loads(i)
                        for s in range(2):
                            sp.wait_ge(S["mod_c_done"], i * 2 + s - 1)
                            sp.dma_start(mod_c_ring[:, s, :], mod_rows[i * 2 + (MOD_A + MOD_B + s)]
                                         ).then_inc(mod_c_ld[s], 16)
                with sp.Fori(max(rounds, 1), EXPERT_TILES // RING) as i:
                    expert_loads(i)
                at = first + EXPERT_TILES // RING
            for k in range(KC):
                sp.wait_ge(S["out_ready"], k + 1)
                sp.dma_start(out[:, k, :], sq[:, k, :]).then_inc(S["stored"], 16)
            sp.wait_ge(S["stored"], 16 * KC)

        @block.gpsimd
        def _(pool):
            nc.gpsimd.memset(ones[:], 1.0)
            nc.gpsimd.iota(iota_i[:], [[1, P]], base=0, channel_multiplier=0)
            nc.gpsimd.memset(ident[:], 0.0).then_inc(S["pool_chain"], 1)
            pool.wait_ge(S["pool_chain"], 1)
            nc.gpsimd.affine_select(out=ident[:], in_=ident[:], compare_op=ALU.not_equal, fill=1.0, base=0,
                                    pattern=[[-1, P]], channel_multiplier=1).then_inc(S["consts"], 1)

            def make_lo(grp, s):
                pool.wait_ge(S["hi_ready"], grp * RING + s + 1)
                nc.gpsimd.tensor_tensor(lo_of(grp, s), w_raw[:, s, :], hi_of(grp, s).bitcast(F32), ALU.subtract
                                        ).then_inc(S["lo_ready"], 1)

            for s in range(RING):
                make_lo(0, s)
            pool.wait_ge(S["late_inputs"], 16 * N_LATE_INPUTS)
            nc.gpsimd.affine_select(out=ws[:], in_=ws[:], compare_op=ALU.is_ge, fill=0.0, base=0,
                                    pattern=[[0, AC], [1, P]], channel_multiplier=-1).then_inc(S["ws_ready"], 1)
            mixer_out = BASE["ev_out"] // RING
            for g in range(RING, EV_IN):
                make_lo(g // RING, g % RING)
                m = g - MOD_G_LAG
                if 0 <= m < MOD_G:
                    tile = mod_b_ring[m % MOD_B_RING]
                    pool.wait_ge(mod_b_ld[m % MOD_B_RING], 16 * (m // MOD_B_RING + 1))
                    nc.gpsimd.tensor_tensor(tile, tile, c_row[:], ALU.mult).then_inc(S["mod_g_prod"], 1)
            for s in range(RING):
                if s == 2:
                    for c in range(AC):
                        pool.wait_ge(S["hh_ready"], KC + c + 1)
                        nc.gpsimd.tensor_tensor(h_lo[:, c, :], conv[:, c, :], h_hi[:, c, :].bitcast(F32), ALU.subtract
                                                ).then_inc(S["hl_ready"], 1)
                make_lo(mixer_out, s)
            at = mixer_out + 1
            for pair in PAIRS[2:] + [TILES]:
                with pool.Fori(at, pair // RING) as i:
                    for s in range(RING):
                        make_lo(i, s)
                if pair < TILES:
                    for s in range(RING):
                        make_lo(pair // RING, s)
                at = pair // RING + 1

        @block.scalar
        def _(act):
            chain = [0]

            def link(ins):
                chain[0] += 1
                ins.then_inc(S["act_chain"], 1)
                act.wait_ge(S["act_chain"], chain[0])

            def make_hi(grp, s, first=False, last_user=2):
                grp, s = grp + s // RING, s % RING
                act.wait_ge(ld[s], grp * 16 + 16)
                if not first:
                    act.wait_ge(S["tile_done"], grp * RING + (s - last_user + 1))
                nc.scalar.activation(hi_of(grp, s), w_raw[:, s, :], ACT.Copy).then_inc(S["hi_ready"], 1)

            def make_third_hi(name):
                make_hi(BASE[name] // RING, 2, name == "ev_in", last_user=4)

            def evacuate(grp, s, dst, func, bank, **kw):
                act.wait_ge(S["tile_done"], grp * RING + s + 1)
                nc.scalar.activation(dst, ps[bank][:], func, **kw).then_inc(S["evac"], 1)

            def step(g, dst, func, **kw):
                evacuate(g // RING, g % RING, dst, func, g % 2, **kw)
                if g not in PAIRS:
                    make_hi(g // RING, g % RING + 2)

            def square(k):
                nc.scalar.activation(sq[:, k, :], x[:, k, :], ACT.Square).then_inc(S["sq_ready"], 1)

            def norm_act(n, shift):
                if n and n not in RESIDUAL:
                    for k in range(KC):
                        act.wait_ge(S["x_ready"], XR[n] - KC + k + 1)
                        square(k)
                if shift is None:
                    return
                make_third_hi(("ev_in", "q0", "od_in", "q1")[n])
                if n == 0:
                    act.wait_ge(S["mod_ready"], 1)
                for k in range(KC):
                    act.wait_ge(S["t_ready"], n * KC + k + 1)
                    nc.scalar.activation(h_hi[:, k, :], sq[:, k, :], ACT.Identity, bias=shift(k)
                                         ).then_inc(S["hh_ready"], 1)

            def ln_squares(m, src):
                for c in range(AC):
                    act.wait_ge(S["centred"], m * AC + c + 1)
                    nc.scalar.activation(ln_sq[m][:, c, :], src[:, c, :], ACT.Square).then_inc(S["ln_sqd"], 1)

            def residual_act(name, l):
                base, had = BASE[name], XR[{"ev_out": 0, "od_out": 2}[name]]
                for k in range(KC):
                    step(base + k, y_slot[:, k % 2, :], ACT.Identity, scale=modc(l, 2, k))
                    if k:
                        act.wait_ge(S["x_ready"], had + k)
                        square(k - 1)
                act.wait_ge(S["x_ready"], had + KC)
                square(KC - 1)

            def peer_act(l):
                base = BASE[f"q{l}"]
                for i in range(Q_TILES):
                    step(base + i, q[:, i, :], ACT.Copy)
                for grp in range(TB * 4):
                    act.wait_ge(S["sc_mm"], l * TB * 4 + grp + 1)
                    nc.scalar.copy(scores[:, grp // 4, 4 * (grp % 4):4 * (grp % 4) + 4, :],
                                   ps[2 + grp % 2][:].rearrange("p (a b) -> p a b", a=4)
                                   ).then_inc(S["sc_ev"], 1)
                first = BASE[f"u{l}"] // RING

                def expert_step(grp, s, before=None):
                    rounds = grp + l * EXPERT_TILES // RING
                    if not (isinstance(grp, int) and grp == 0 and l == 0):
                        act.wait_ge(act_st[s], rounds * 16)
                    if before:
                        before()
                    evacuate(grp + first, s, act_ring[:, s, :], ACT.Gelu, s % 2)
                    make_hi(grp + first, s + 2)
                    act.wait_ge(S["evac"], EVAC[f"u{l}"] + grp * RING + s + 1)
                    act.dma_start(act_dram[grp * RING + s], act_ring[:, s, :]).then_inc(act_st[s], 16)

                per = TILES_PER_BLOCK // RING

                def block_steps(b, skip=0):
                    for r in range(skip, per):
                        if r == per - 1:
                            act.wait_ge(S["exp_in"], l * TB + b + 1)
                            nc.scalar.activation(gate[:], best_v[:], ACT.Exp).then_inc(S["exp_out"], 1)
                        for s in range(RING):
                            expert_step(b * per + r, s)

                for s in range(RING):
                    expert_step(0, s)
                block_steps(0, 1)
                with act.Fori(1, TB) as b:
                    block_steps(b)
                at = TB * per
                for s in range(RING):
                    expert_step(at, s)
                at += 1
                with act.Fori(0, TB) as b:
                    for half in range(2):
                        act.wait_ge(g_st[half], b * 16 + (l * TB + 1) * 16)
                        with act.Fori(0, HALF // GROUP // RING) as r:
                            for s in range(RING):
                                expert_step(b * 4 + half * 2 + r + at, s)
                                for w in range(2):
                                    act.wait_ge(S["g_mm"], b * 32 + r * 8 + (l * 2 * T // GROUP + half * 16 + 2 * s + w + 1))
                                    nc.scalar.copy(
                                        gate_st[:, half, :, bass.ds(r * (RING * GROUP) + (s * GROUP + 4 * w), 4)]
                                        .rearrange("p j t -> p t j"),
                                        ps[2 + w][:].rearrange("p (t j) -> p t j", t=4)).then_inc(S["g_ev"], 1)
                        act.wait_ge(S["g_ev"], b * 32 + (l * 2 * T // GROUP + half * 16 + 16 + 2))
                        act.dma_start(gate_dram[b * 2 + half], gate_st[:, half, :, :]).then_inc(g_st[half], 16)
                at += T // GROUP // RING
                with act.Fori(at, EXPERT_TILES // RING - 1) as i:
                    for s in range(RING):
                        expert_step(i, s)

                v_first = BASE[f"v{l}"] // RING

                def prod_hi(grp, s, head=False):
                    grp, s = grp + s // RING, s % RING
                    act.wait_ge(S["p_ready"], grp * RING + (l * EXPERT_TILES + s + 1))
                    if not head:
                        act.wait_ge(S["tile_done"], (grp + v_first) * RING + s - 1)
                    nc.scalar.activation(h_hi[:, s % 2, :], prod[:, s % 2, :], ACT.Copy).then_inc(S["ph_ready"], 1)

                def first_prod_hi():
                    act.wait_ge(S["tile_done"], BASE[f"v{l}"])
                    prod_hi(0, 0, True)

                last = EXPERT_TILES // RING - 1
                for s in range(RING):
                    expert_step(last, s, first_prod_hi if s == RING - 1 else None)
                with act.Fori(0, last) as i:
                    for s in range(RING):
                        prod_hi(i, s + 1)
                        make_hi(i + v_first, s + 2)
                for s in range(RING):
                    if s < RING - 1:
                        prod_hi(last, s + 1)
                    if (last + v_first) * RING + s + 2 < TILES:
                        make_hi(last + v_first, s + 2)

            act.dma_start(cols[:], cols_in).then_inc(S["inputs"], 16)
            for half in range(2):
                act.sem_inc(g_st[half], 16)
            act.sem_inc(S["g_ev"], 2)
            act.wait_ge(S["c_in"], 16)
            nc.scalar.activation(c_row[:], c_row[:], ACT.Silu).then_inc(S["c_ready"], 1)
            act.wait_ge(S["inputs"], 16 * N_INPUTS)

            for k in range(KC):
                square(k)
            make_hi(0, 0, True)
            make_hi(0, 1, True)
            norm_act(0, lambda k: modc(0, 0, k))
            for g in range(EV_IN):
                c, which = g // 2, g % 2
                if c < AC:
                    step(g, glu_in(c, which), (ACT.Copy, ACT.Sigmoid)[which])
                elif g < 3 * AC:
                    step(g, v_c[:, g - 2 * AC, :], ACT.Gelu)
                else:
                    step(g, u_c[:, g - 3 * AC, :], ACT.Gelu)
                m = g - MOD_G_LAG
                if 0 <= m < MOD_G:
                    act.wait_ge(S["mod_g_prod"], m + 1)
                    tile = mod_b_ring[m % MOD_B_RING]
                    nc.scalar.activation(tile, tile, ACT.Copy, accum_out=mod[:, MOD_A + m:MOD_A + m + 1]
                                         ).then_inc(S["mod_b_done"], 1)
                if g == EV_IN - 2:
                    ln_squares(0, v_c)

            make_third_hi("ev_out")
            ln_squares(1, conv)
            for c in range(AC):
                act.wait_ge(S["scaled"], c + 1)
                nc.scalar.activation(v_c[:, c, :], v_c[:, c, :], ACT.Identity, bias=col("gln_b", c)
                                     ).then_inc(S["ln_out"], 1)
            for c in range(AC):
                act.wait_ge(S["v_tr"], c + 1)
                nc.scalar.copy(v_tok[:, c, :], ps[2 + c % 2][:]).then_inc(S["v_tok_ready"], 1)
            for c in range(AC):
                act.wait_ge(S["scaled"], AC + c + 1)
                ins = nc.scalar.activation(conv[:, c, :], conv[:, c, :], ACT.Silu, bias=col("cln_b", c))
            link(ins)
            for c in range(AC):
                nc.scalar.activation(h_hi[:, c, :], conv[:, c, :], ACT.Copy).then_inc(S["hh_ready"], 1)
            for c in range(AC):
                act.wait_ge(S["bout"], c + 1)
                nc.scalar.activation(h_hi[:, AC + c, :], u_c[:, c, :], ACT.Copy).then_inc(S["hh_ready"], 1)
            act.wait_ge(S["mod_ready"], 2)
            residual_act("ev_out", 0)
            norm_act(1, lambda k: modc(0, 3, k))
            peer_act(0)

            norm_act(2, lambda k: modc(1, 0, k))
            for c in range(KC):
                g = BASE["od_in"] + 3 * c
                if c >= 1:
                    act.wait_ge(S["z_free"], c)
                for w in range(3):
                    evacuate((g + w) // RING, (g + w) % RING, zc[:, w, :], ACT.Copy, (g + w) % 2)
                    if g + w not in PAIRS:
                        make_hi((g + w) // RING, (g + w) % RING + 2)
            make_third_hi("od_out")
            for c in range(KC):
                act.wait_ge(S["z_free"], c + 1)
                nc.scalar.activation(h_hi[:, c, :], y_c[:, c, :], ACT.Copy).then_inc(S["hh_ready"], 1)
            residual_act("od_out", 1)
            norm_act(3, lambda k: modc(1, 3, k))
            peer_act(1)
            norm_act(4, None)

        @block.vector
        def _(dve):
            chain = [0]

            def link(ins, plus=0):
                chain[0] += 1
                ins.then_inc(S["dve_chain"], 1)
                dve.wait_ge(S["dve_chain"], plus + chain[0])

            V = nc.vector

            def take_diagonal(m, bank, width):
                for b in range(TB):
                    ins = V.scalar_tensor_tensor(out=stat[:, 2 + m, b * P:(b + 1) * P],
                                                 in0=ps[bank][:, b * P:(b + 1) * P], scalar=1.0 / width, in1=ident[:],
                                                 op0=ALU.mult, op1=ALU.mult,
                                                 accum_out=var_c[:, m * TB + b:m * TB + b + 1])
                return ins

            def inverse_roots(norms):
                n = norms * TB
                v, r, t = var_c[:, 0:n], root_c[:, 0:n], root_t[:, 0:n]
                link(V.tensor_scalar(v, v, EPS, None, ALU.add))
                link(V.tensor_scalar(r.bitcast(I32), v.bitcast(I32), 1, None, ALU.logical_shift_right))
                link(V.tensor_scalar(r.bitcast(I32), r.bitcast(I32), -1.0, float(0x5F3759DF), ALU.mult, ALU.add))
                for _ in range(3):
                    link(V.tensor_tensor(t, r, r, ALU.mult))
                    link(V.scalar_tensor_tensor(out=t, in0=t, scalar=-0.5, in1=v, op0=ALU.mult, op1=ALU.mult))
                    link(V.scalar_tensor_tensor(out=r, in0=t, scalar=1.5, in1=r, op0=ALU.add, op1=ALU.mult))
                for m in range(norms):
                    for b in range(TB):
                        ins = V.tensor_scalar(stat[:, m, b * P:(b + 1) * P], ident[:],
                                              root_c[:, m * TB + b:m * TB + b + 1], None, ALU.mult)
                    ins.then_inc(S["diag_ready"], 1)

            def norm_root(n):
                dve.wait_ge(S["ssum"], n + 1)
                link(take_diagonal(0, 5, D))
                inverse_roots(1)

            def norm_dve(n, gain_col, shift):
                if n:
                    norm_root(n)
                    dve.wait_ge(S["inv_ready"], ROOTS_BEFORE[n] + 1)
                for k in range(KC + 2):
                    if k < KC and n:
                        V.scalar_tensor_tensor(out=sq[:, k, :], in0=x[:, k, :], scalar=gain_col(k),
                                               in1=ps[5][:], op0=ALU.mult, op1=ALU.mult
                                               ).then_inc(S["t_ready"] if shift else S["out_ready"], 1)
                    if k >= 2 and shift:
                        c = k - 2
                        dve.wait_ge(S["hh_ready"], HR[n] + c + 1)
                        V.scalar_tensor_tensor(out=h_lo[:, c, :], in0=sq[:, c, :], scalar=shift(c),
                                               in1=h_hi[:, c, :].bitcast(F32), op0=ALU.add, op1=ALU.subtract
                                               ).then_inc(S["hl_ready"], 1)

            def ln_centre(m, src):
                dve.wait_ge(S["ln_mm"], 2 * m + 1)
                link(V.tensor_scalar(stat[:, m, :], ps[ln_bank[m]][:], 1.0 / (AC * P), None, ALU.mult))
                for c in range(AC):
                    V.tensor_tensor(src[:, c, :], src[:, c, :], stat[:, m, :], ALU.subtract
                                    ).then_inc(S["centred"], 1)

            def ln_scale(m, src, gain_name):
                dve.wait_ge(S["inv_ready"], ROOTS_BEFORE[1] - 2 + m + 1)
                for c in range(AC):
                    V.scalar_tensor_tensor(out=src[:, c, :], in0=src[:, c, :], scalar=col(gain_name, c),
                                           in1=ps[ln_bank[m]][:], op0=ALU.mult, op1=ALU.mult
                                           ).then_inc(S["scaled"], 1)

            def mod_row_sum(w, dst):
                return V.scalar_tensor_tensor(out=w, in0=w, scalar=1.0, in1=c_row[:], op0=ALU.mult, op1=ALU.mult,
                                              accum_out=dst)

            def mod_b(m):
                s = m % MOD_B_RING
                dve.wait_ge(mod_b_ld[s], 16 * (m // MOD_B_RING + 1))
                mod_row_sum(mod_b_ring[s], mod[:, MOD_A + m:MOD_A + m + 1]).then_inc(S["mod_b_done"], 1)

            def residual_dve(name):
                for k in range(KC):
                    if name == "ev_out":
                        mod_b(MOD_G + 2 * k)
                        mod_b(MOD_G + 2 * k + 1)
                    dve.wait_ge(S["evac"], EVAC[name] + k + 1)
                    V.tensor_tensor(x[:, k, :], x[:, k, :], y_slot[:, k % 2, :], ALU.add).then_inc(S["x_ready"], 1)

            def peer_dve(l):
                LINKS = 20
                base = chain[0]
                with dve.Fori(0, TB) as b:
                    plus = b * LINKS

                    def chained(ins):
                        link(ins, plus)

                    def then_top(ins):
                        link(ins, plus)
                        dve.sem_inc(S["top_step"], 1)

                    dve.wait_ge(S["sc_ev"], (l + 1) * TB * 4)
                    then_top(V.tensor_copy(work[:], scores[:, bass.ds(b, 1), :, :].rearrange("p o a b -> p (o a) b")))
                    for hp in range(2 * HEADS):
                        ins = V.max(top_v[:, hp, 0:8], work[:, hp, :])
                    then_top(ins)
                    for hp in range(2 * HEADS):
                        V.max_index(top_i[:, hp, 0:8], top_v[:, hp, 0:8], work[:, hp, :])
                        ins = V.match_replace(work2[:, hp, :], top_v[:, hp, 0:8], work[:, hp, :], LOWEST)
                    then_top(ins)
                    for hp in range(2 * HEADS):
                        ins = V.max(top_v[:, hp, 8:16], work2[:, hp, :])
                    then_top(ins)
                    for hp in range(2 * HEADS):
                        ins = V.max_index(top_i[:, hp, 8:16], top_v[:, hp, 8:16], work2[:, hp, :])
                    then_top(ins)
                    chained(V.tensor_copy(top_f[:], top_i[:]))
                    f4 = top_f[:].rearrange("p (h two) k -> p h two k", two=2)
                    v4 = top_v[:].rearrange("p (h two) k -> p h two k", two=2)
                    chained(V.tensor_scalar(f4[:, :, 0, :], f4[:, :, 0, :], float(NK), None, ALU.mult))
                    for dst, src in ((cand, v4), (code, f4)):
                        for (a, n), o in zip(ROWS, OFFS):
                            V.tensor_tensor(dst[:, :, o:o + n], src[:, :, 1, 0:n],
                                            src[:, :, 0, a:a + 1].to_broadcast([P, HEADS, n]), ALU.add)
                        ins = V.tensor_tensor(dst[:, :, OFFS[-1]:], src[:, :, 0, 8:16],
                                              src[:, :, 1, 0:1].to_broadcast([P, HEADS, 8]), ALU.add)
                    then_top(ins)
                    for h in range(HEADS):
                        ins = V.max(best_v[:, h, 0:8], cand[:, h, :])
                    then_top(ins)
                    for h in range(HEADS):
                        V.max_index(best_i[:, h, 0:8], best_v[:, h, 0:8], cand[:, h, :])
                        ins = V.match_replace(cand2[:, h, :], best_v[:, h, 0:8], cand[:, h, :], LOWEST)
                    then_top(ins)
                    for h in range(HEADS):
                        ins = V.max(best_v[:, h, 8:16], cand2[:, h, :])
                    then_top(ins)
                    for h in range(HEADS):
                        ins = V.max_index(best_i[:, h, 8:16], best_v[:, h, 8:16], cand2[:, h, :])
                    then_top(ins)
                    chained(V.tensor_copy(best_f[:], best_i[:]))
                    chained(V.tensor_copy(gate_z[:], best_v[:, :, 0:1].rearrange("p h o -> p (h o)")))
                    V.tensor_tensor(best_v[:], best_v[:], gate_z[:].unsqueeze(2).to_broadcast([P, HEADS, TOPK]),
                                    ALU.subtract).then_inc(S["exp_in"], 1)
                    for h in range(HEADS):
                        V.tensor_tensor(pick[:], best_f[:, h, :].unsqueeze(2).to_broadcast([P, TOPK, NCAND]),
                                        iota_f[:, 0:NCAND].unsqueeze(1).to_broadcast([P, TOPK, NCAND]),
                                        ALU.is_equal).then_inc(S["topk"], 1)
                        dve.wait_ge(S["topk"], b * 24 + (l * TB * 24 + 3 * h + 1))
                        V.tensor_tensor(pick[:], pick[:], code[:, h, :].unsqueeze(1).to_broadcast([P, TOPK, NCAND]),
                                        ALU.mult).then_inc(S["topk"], 1)
                        dve.wait_ge(S["topk"], b * 24 + (l * TB * 24 + 3 * h + 2))
                        V.tensor_reduce(best_e[:, h, :], pick[:], AX_X, ALU.add).then_inc(S["topk"], 1)
                        dve.wait_ge(S["topk"], b * 24 + (l * TB * 24 + 3 * h + 3))
                    chained(V.tensor_copy(expert[:], best_e[:].rearrange("p h k -> p (h k)")))
                    V.tensor_scalar(expert_i[:], expert[:], 7, None, ALU.logical_shift_right)
                    chained(V.tensor_scalar(expert_j[:], expert[:], NK - 1, None, ALU.bitwise_and))
                    V.tensor_copy(i_f[:], expert_i[:])
                    chained(V.tensor_copy(j_f[:], expert_j[:]))
                    dve.wait_ge(S["exp_out"], b + (l * TB + 1))
                    chained(V.tensor_reduce(gate_z[:], gate[:], AX_X, ALU.add))
                    chained(V.reciprocal(gate_z[:], gate_z[:]))
                    V.tensor_tensor(gate[:], gate[:], gate_z[:].unsqueeze(2).to_broadcast([P, HEADS, TOPK]),
                                    ALU.mult).then_inc(S["tr_read"], 1)
                    dve.wait_ge(S["tr_mm"], b + (l * TB + 1))
                    V.tensor_copy(i_t[:, bass.ds(b * P, P)], ps[4][:, 0:P])
                    V.tensor_copy(j_t[:, bass.ds(b * P, P)], ps[4][:, P:2 * P])
                    chained(V.tensor_copy(gate_t[:, 2, bass.ds(b * P, P)], ps[4][:, 2 * P:3 * P]))
                    assert chain[0] - base == LINKS, chain[0] - base
                chain[0] = base + TB * LINKS
                for part_no in range(2):
                    link(V.tensor_copy(gate_bf[:], gate_t[:, 2, :]))
                    link(V.tensor_copy(gate_t[:, part_no, :], gate_bf[:]))
                    link(V.tensor_tensor(gate_t[:, 2, :], gate_t[:, 2, :], gate_t[:, part_no, :], ALU.subtract))
                groups = l * T // GROUP

                def one_hots(r, s, head):
                    if not head:
                        dve.wait_ge(S["g_mm"], r * 4 + (2 * (groups + s) - 2))
                    V.tensor_tensor(oh_i[:, s, :, :], iota_bf[:].unsqueeze(1).to_broadcast([P, GROUP, NK]),
                                    i_t[:, bass.ds(r * (2 * GROUP) + s * GROUP, GROUP)].unsqueeze(2)
                                    .to_broadcast([P, GROUP, NK]), ALU.is_equal)
                    for n in range(GROUP):
                        t = bass.ds(r * (2 * GROUP) + (s * GROUP + n), 1)
                        for w in range(3):
                            ins = V.tensor_scalar(oh_j[:, s, n, w, :], iota_bf[:], j_t[:, t], gate_t[:, w, t],
                                                  ALU.is_equal, ALU.mult)
                    ins.then_inc(S["oh_ready"], 1)

                for s in range(2):
                    one_hots(0, s, l == 0)
                with dve.Fori(1, T // GROUP // 2) as r:
                    for s in range(2):
                        one_hots(r, s, False)

                first = BASE[f"v{l}"]

                def gated(grp, s, head=False):
                    grp, s = grp + s // RING, s % RING
                    dve.wait_ge(act_ld[s], grp * 16 + (l * EXPERT_TILES // RING + 1) * 16)
                    dve.wait_ge(g_ld[s], grp * 16 + (l * EXPERT_TILES // RING + 1) * 16)
                    if not head:
                        dve.wait_ge(S["pl_ready"], grp * RING + (l * EXPERT_TILES + s - 1))
                    V.tensor_tensor(prod[:, s % 2, :], act_ring[:, s, :], g_ring[:, s, :], ALU.mult
                                    ).then_inc(S["p_ready"], 1)

                def prod_lo(grp, s):
                    dve.wait_ge(S["ph_ready"], grp * RING + (l * EXPERT_TILES + s + 1))
                    V.tensor_tensor(h_lo[:, s % 2, :], prod[:, s % 2, :], h_hi[:, s % 2, :].bitcast(F32),
                                    ALU.subtract).then_inc(S["pl_ready"], 1)

                gated(0, 0, True)
                gated(0, 1, True)
                last = EXPERT_TILES // RING - 1

                def products(i):
                    for s in range(RING):
                        prod_lo(i, s)
                        gated(i, s + 2)

                rounds = 0
                if l == 0:
                    rounds = MOD_C_ROUNDS
                    with dve.Fori(0, rounds) as i:
                        products(i)
                        for s in range(2):
                            dve.wait_ge(mod_c_ld[s], i * 16 + 16)
                            mod_row_sum(mod_c_ring[:, s, :], mod[:, bass.ds(i * 2 + (MOD - MOD_C + s), 1)]
                                        ).then_inc(S["mod_c_done"], 1)
                with dve.Fori(rounds, last) as i:
                    products(i)
                if l == 0:
                    dve.wait_ge(S["mod_c_done"], MOD_C)
                    add_bias(MOD_A + MOD_B, MOD_C, mod[:, MOD_A + MOD_B:MOD])
                    norm_gain(2)
                    norm_gain(3).then_inc(S["mod_ready"], 1)
                    dve.wait_ge(S["mod_ready"], 4)
                for s in range(RING):
                    prod_lo(last, s)
                    if s < 2:
                        gated(last, s + 2)
                for k in range(KC):
                    if k < KC - 1:
                        dve.wait_ge(S["bank_done"], l * (KC - 1) + k + 1)
                    else:
                        dve.wait_ge(S["tile_done"], first + EXPERT_TILES)
                    ins = V.scalar_tensor_tensor(out=x[:, k, :], in0=out_bank(k), scalar=modc(l, 5, k), in1=x[:, k, :],
                                                 op0=ALU.mult, op1=ALU.add)
                    ins.then_inc(S["x_ready"], 1)

            def add_bias(at, n, src):
                link(V.tensor_tensor(mod[:, at:at + n], src, cols[:, COLS["mod_b"] + at:COLS["mod_b"] + at + n],
                                     ALU.add))

            def norm_gain(n):
                l, which = n // 2, n % 2
                at = l * 6 * KC + (1 + 3 * which) * KC
                name = COLS[("norm1_g", "norm2_g")[which]] + l * KC
                return V.scalar_tensor_tensor(out=gain[:, n, :], in0=mod[:, at:at + KC], scalar=1.0,
                                              in1=cols[:, name:name + KC], op0=ALU.add, op1=ALU.mult)

            def mod_a(i):
                m = MOD_A_ORDER[i]
                dve.wait_ge(mod_a_ld[i % MOD_A_RING], 16 * (i // MOD_A_RING + 1))
                mod_row_sum(mod_a_ring[:, i % MOD_A_RING, :], mod[:, m:m + 1]).then_inc(S["mod_a_done"], 1)

            dve.wait_ge(S["consts"], 1)
            V.tensor_copy(iota_bf[:], iota_i[:])
            V.tensor_copy(iota_f[:], iota_i[:])
            dve.wait_ge(S["inputs"], 16 * N_INPUTS)
            dve.wait_ge(S["c_ready"], 1)
            for i in range(KC):
                mod_a(i)
            norm_root(0)
            dve.wait_ge(S["mod_a_done"], KC)
            add_bias(KC, KC, mod[:, KC:2 * KC])
            link(norm_gain(0))
            mod_a(KC)
            dve.wait_ge(S["inv_ready"], 1)
            for k in range(KC):
                V.scalar_tensor_tensor(out=sq[:, k, :], in0=x[:, k, :], scalar=gain[:, 0, k:k + 1], in1=ps[5][:],
                                       op0=ALU.mult, op1=ALU.mult).then_inc(S["t_ready"], 1)
            for i in range(KC + 1, 2 * KC):
                mod_a(i)
            dve.wait_ge(S["mod_a_done"], MOD_A)
            add_bias(0, KC, mod[:, 0:KC])
            dve.sem_inc(S["mod_ready"], 1)

            norm_dve(0, None, lambda k: modc(0, 0, k))
            dve.wait_ge(S["hl_ready"], KC)
            link(V.memset(a_pad[:, :, 0:PAD], 0.0))

            def convolve(c):
                dve.wait_ge(S["evac"], 2 * c + 2)
                V.tensor_tensor(a_pad[:, c, PAD:PAD + T], glu_in(c, 0), glu_in(c, 1), ALU.mult
                                ).then_inc(S["glu_done"], 1)
                dve.wait_ge(S["glu_done"], c + 1)
                sums = (conv[:, c, :], odd_taps[:, 0, :])
                V.tensor_scalar(sums[0], a_pad[:, c, 0:T], col("conv_w", c * TAPS), col("conv_b", c),
                                ALU.mult, ALU.add).then_inc(S["tap"], 1)
                V.tensor_scalar(sums[1], a_pad[:, c, 1:1 + T], col("conv_w", c * TAPS + 1), None,
                                ALU.mult).then_inc(S["tap"], 1)
                for tap in range(2, TAPS):
                    dve.wait_ge(S["tap"], c * TAPS + tap - 1)
                    V.scalar_tensor_tensor(out=sums[tap % 2], in0=a_pad[:, c, tap:tap + T],
                                           scalar=col("conv_w", c * TAPS + tap), in1=sums[tap % 2],
                                           op0=ALU.mult, op1=ALU.add).then_inc(S["tap"], 1)
                dve.wait_ge(S["tap"], (c + 1) * TAPS)
                V.tensor_tensor(sums[0], sums[0], sums[1], ALU.add).then_inc(S["conv_done"], 1)
                dve.wait_ge(S["conv_done"], c + 1)

            for c in range(AC):
                if c == AC - 1:
                    ln_centre(0, v_c)
                convolve(c)
            ln_centre(1, conv)
            dve.wait_ge(S["centred"], 2 * AC)
            for m in range(2):
                dve.wait_ge(S["ln_mm"], 2 * m + 2)
                ins = take_diagonal(m, ln_bank[m], AC * P)
            link(ins)
            inverse_roots(2)
            ln_scale(0, v_c, "gln_g")
            ln_scale(1, conv, "cln_g")
            dve.wait_ge(S["mod_b_done"], MOD_G)
            add_bias(MOD_A, MOD_G, mod[:, MOD_A:MOD_A + MOD_G])
            dve.sem_inc(S["mod_ready"], 1)
            dve.wait_ge(S["ws_ready"], 1)
            for c in range(AC):
                dve.wait_ge(S["mixed"], c + 1)
                V.tensor_tensor(z[:, c % 2, :].rearrange("p (n t) -> p n t", t=P),
                                ps[6 + c % 2][:].rearrange("p (n t) -> p n t", t=P),
                                bs[:, c:c + 1, :].to_broadcast([P, T // P, P]), ALU.add).then_inc(S["mixed_read"], 1)
                dve.wait_ge(S["mixed_read"], c + 1)
                V.tensor_tensor(u_c[:, c, :], u_c[:, c, :], z[:, c % 2, :], ALU.mult).then_inc(S["bout"], 1)
            dve.wait_ge(S["hl_ready"], KC + AC)
            for c in range(AC, KC):
                dve.wait_ge(S["hh_ready"], KC + c + 1)
                V.tensor_tensor(h_lo[:, c, :], u_c[:, c - AC, :], h_hi[:, c, :].bitcast(F32), ALU.subtract
                                ).then_inc(S["hl_ready"], 1)
            residual_dve("ev_out")
            dve.wait_ge(S["mod_b_done"], MOD_B)
            add_bias(MOD_A + MOD_G, MOD_B - MOD_G, mod[:, MOD_A + MOD_G:MOD_A + MOD_B])
            norm_gain(1).then_inc(S["mod_ready"], 1)
            dve.wait_ge(S["mod_ready"], 3)
            norm_dve(1, lambda k: gain[:, 1, k:k + 1], lambda k: modc(0, 3, k))
            peer_dve(0)

            norm_dve(2, lambda k: gain[:, 2, k:k + 1], lambda k: modc(1, 0, k))
            dve.wait_ge(S["hl_ready"], HR[2] + KC)
            link(V.memset(m_pad[:, :, 0:2], 0.0))
            for c in range(KC):
                m = c % 2
                dve.wait_ge(S["evac"], EVAC["od_in"] + 3 * c + 3)
                link(V.tensor_tensor(m_pad[:, m, 2:2 + T], zc[:, 0, :], zc[:, 1, :], ALU.mult))
                link(V.tensor_scalar(y_c[:, c, :], m_pad[:, m, 0:T], col("od_conv_w", 3 * c), None, ALU.mult))
                for k in (1, 2):
                    link(V.scalar_tensor_tensor(out=y_c[:, c, :], in0=m_pad[:, m, k:k + T],
                                                scalar=col("od_conv_w", 3 * c + k), in1=y_c[:, c, :],
                                                op0=ALU.mult, op1=ALU.add))
                V.tensor_tensor(y_c[:, c, :], y_c[:, c, :], zc[:, 2, :], ALU.mult).then_inc(S["z_free"], 1)
            dve.wait_ge(S["z_free"], KC)
            for c in range(KC):
                dve.wait_ge(S["hh_ready"], 3 * KC + KC + c + 1)
                V.tensor_tensor(h_lo[:, c, :], y_c[:, c, :], h_hi[:, c, :].bitcast(F32), ALU.subtract
                                ).then_inc(S["hl_ready"], 1)
            residual_dve("od_out")
            norm_dve(3, lambda k: gain[:, 3, k:k + 1], lambda k: modc(1, 3, k))
            peer_dve(1)
            norm_dve(4, lambda k: col("final_g", k), None)

        @block.tensor
        def _(pe):
            MM = nc.tensor.matmul

            def operands_ready(grp, s):
                pe.wait_ge(S["hi_ready"], grp * RING + s + 1)
                pe.wait_ge(S["lo_ready"], grp * RING + s + 1)

            def project(grp, s, banked):
                operands_ready(grp, s)
                pe.wait_ge(S["evac"], banked - 1)
                o = ps[s % 2][:]
                for k in range(KC):
                    hi = w_hi[:, s % 2, k * P:(k + 1) * P]
                    lo = w_lo[:, s % 2, k * P:(k + 1) * P]
                    MM(o, hi, h_hi[:, k, :], start=(k == 0), stop=False)
                    MM(o, lo, h_hi[:, k, :], start=False, stop=False)
                    ins = MM(o, hi, h_lo[:, k, :], start=False, stop=(k == KC - 1))
                ins.then_inc(S["tile_done"], 1)

            def first_projections(grp, banked, operand):
                for s in range(2):
                    operands_ready(grp, s)
                if banked:
                    pe.wait_ge(S["evac"], banked)
                for k in range(KC):
                    hi = [hi_of(grp, s)[:, k * P:(k + 1) * P] for s in range(2)]
                    lo = [lo_of(grp, s)[:, k * P:(k + 1) * P] for s in range(2)]
                    pe.wait_ge(S["hh_ready"], operand * KC + k + 1)
                    for s in range(2):
                        MM(ps[s][:], hi[s], h_hi[:, k, :], start=(k == 0), stop=False)
                        MM(ps[s][:], lo[s], h_hi[:, k, :], start=False, stop=False)
                    pe.wait_ge(S["hl_ready"], operand * KC + k + 1)
                    for s in range(2):
                        ins = MM(ps[s][:], hi[s], h_lo[:, k, :], start=False, stop=(k == KC - 1))
                        if k == KC - 1:
                            ins.then_inc(S["tile_done"], 1)

            def projections(name, n, operand):
                g, b = BASE[name] // RING, EVAC[name]
                first_projections(g, b, operand)
                for s in range(2, RING):
                    project(g, s, b + s)
                with pe.Fori(1, n // RING) as i:
                    for s in range(RING):
                        project(i + g, s, i * RING + (b + s))

            def projections_and_squares(name, operand, n):
                g, b = BASE[name] // RING, EVAC[name]
                first_projections(g, b, operand)
                for k in range(2, KC + 2):
                    if k < KC:
                        project(g + k // RING, k % RING, b + k)
                    square_sum(n, k - 2)

            def square_sum(n, k):
                pe.wait_ge(S["sq_ready"], n * KC + k + 1)
                ins = MM(ps[5][:], ones[:], sq[:, k, :], start=(k == 0), stop=(k == KC - 1))
                if k == KC - 1:
                    ins.then_inc(S["ssum"], 1)
                    spread_roots(ROOTS_BEFORE[n], 5)

            def spread_roots(done, bank, m=0):
                pe.wait_ge(S["diag_ready"], done + 1)
                for b in range(TB):
                    ins = MM(ps[bank][:, b * P:(b + 1) * P], ones[:], stat[:, m, b * P:(b + 1) * P],
                             start=True, stop=True)
                ins.then_inc(S["inv_ready"], 1)

            def sum_squares(n):
                for k in range(KC):
                    square_sum(n, k)

            def ln_sum(m, src, ready, had):
                for c in range(AC):
                    pe.wait_ge(ready, had + c + 1)
                    ins = MM(ps[ln_bank[m]][:], ones[:], src[:, c, :], start=(c == 0), stop=(c == AC - 1))
                ins.then_inc(S["ln_mm"], 1)

            def peer_pe(l):
                projections(f"q{l}", Q_TILES, 2 + 3 * l)
                pe.wait_ge(S["evac"], EVAC[f"u{l}"])
                for grp in range(TB * 4):
                    b = grp // 4
                    if grp >= 2:
                        pe.wait_ge(S["sc_ev"], l * TB * 4 + grp - 1)
                    for w in range(4):
                        hp = 4 * (grp % 4) + w
                        ins = MM(ps[2 + grp % 2][:, w * NK:(w + 1) * NK], q[:, hp, b * P:(b + 1) * P],
                                 sk[:, l, hp % 2, :], start=True, stop=True)
                    ins.then_inc(S["sc_mm"], 1)
                first, banked = BASE[f"u{l}"] // RING, EVAC[f"u{l}"]
                per = TILES_PER_BLOCK // RING
                with pe.Fori(0, TB) as b:
                    with pe.Fori(0, per) as r:
                        for s in range(RING):
                            project(b * per + r + first, s, b * TILES_PER_BLOCK + r * RING + (banked + s))
                    pe.wait_ge(S["tr_read"], b + (l * TB + 1))
                    nc.tensor.transpose(ps[4][:, 0:P], i_f[:], ident[:])
                    nc.tensor.transpose(ps[4][:, P:2 * P], j_f[:], ident[:])
                    nc.tensor.transpose(ps[4][:, 2 * P:3 * P], gate[:].rearrange("p h k -> p (h k)"), ident[:]
                                        ).then_inc(S["tr_mm"], 1)
                at = TB * per
                for s in range(RING):
                    project(at + first, s, banked + at * RING + s)
                at += 1
                groups = l * T // GROUP
                with pe.Fori(0, T // GROUP // RING) as r:
                    for s in range(RING):
                        project(r + (at + first), s, r * RING + (banked + at * RING + s))
                        pe.wait_ge(S["oh_ready"], r * RING + (groups + s + 1))
                        for w in range(2):
                            pe.wait_ge(S["g_ev"], r * 8 + (2 * groups + 2 * s + w + 1))
                            for n in range(4):
                                for p3 in range(3):
                                    ins = MM(ps[2 + w][:, n * NK:(n + 1) * NK], oh_i[:, s % 2, 4 * w + n, :],
                                             oh_j[:, s % 2, 4 * w + n, p3, :], start=(p3 == 0), stop=(p3 == 2))
                            ins.then_inc(S["g_mm"], 1)
                at += T // GROUP // RING
                with pe.Fori(0, EXPERT_TILES // RING - at) as i:
                    for s in range(RING):
                        project(i + (at + first), s, i * RING + (banked + at * RING + s))
                first = BASE[f"v{l}"] // RING
                pe.wait_ge(S["g_ev"], (l + 1) * 2 * T // GROUP + 2)
                pe.wait_ge(S["evac"], banked + EXPERT_TILES - 1)

                def accumulate(grp, s, start, stop):
                    operands_ready(grp + first, s)
                    pe.wait_ge(S["ph_ready"], grp * RING + (l * EXPERT_TILES + s + 1))
                    pe.wait_ge(S["pl_ready"], grp * RING + (l * EXPERT_TILES + s + 1))
                    for k in range(KC):
                        hi = w_hi[:, s % 2, k * P:(k + 1) * P]
                        lo = w_lo[:, s % 2, k * P:(k + 1) * P]
                        if start and k == 4:
                            pe.wait_ge(S["evac"], banked + EXPERT_TILES)
                        MM(out_bank(k), hi, h_hi[:, s % 2, :], start=start, stop=False)
                        MM(out_bank(k), hi, h_lo[:, s % 2, :], start=False, stop=False)
                        ins = MM(out_bank(k), lo, h_hi[:, s % 2, :], start=False, stop=stop)
                        if stop and k < KC - 1:
                            ins.then_inc(S["bank_done"], 1)
                    ins.then_inc(S["tile_done"], 1)

                last = EXPERT_TILES // RING - 1
                for s in range(RING):
                    accumulate(0, s, s == 0, False)
                with pe.Fori(1, last) as i:
                    for s in range(RING):
                        accumulate(i, s, False, False)
                for s in range(RING):
                    accumulate(last, s, False, s == RING - 1)

            pe.wait_ge(S["inputs"], 16 * N_INPUTS)
            pe.wait_ge(S["consts"], 1)
            sum_squares(0)
            first_projections(0, 0, 0)
            for g in range(2, EV_IN):
                project(g // RING, g % RING, g)
                if g == 3 * AC:
                    ln_sum(0, v_c, S["evac"], 2 * AC)
            ln_sum(0, ln_sq[0], S["ln_sqd"], 0)
            ln_sum(1, conv, S["conv_done"], 0)
            ln_sum(1, ln_sq[1], S["ln_sqd"], AC)
            for m in range(2):
                spread_roots(ROOTS_BEFORE[1] - 2 + m, ln_bank[m], m)
            for c in range(AC):
                pe.wait_ge(S["ln_out"], c + 1)
                if c >= 2:
                    pe.wait_ge(S["v_tok_ready"], c - 1)
                for n in range(T // P):
                    ins = nc.tensor.transpose(ps[2 + c % 2][:, n * P:(n + 1) * P], v_c[:, c, n * P:(n + 1) * P],
                                              ident[:])
                ins.then_inc(S["v_tr"], 1)
            pe.wait_ge(S["ws_ready"], 1)
            for c in range(AC):
                pe.wait_ge(S["v_tok_ready"], c + 1)
                if c >= 2:
                    pe.wait_ge(S["mixed_read"], c - 1)
                for n in range(T // P):
                    ins = MM(ps[6 + c % 2][:, n * P:(n + 1) * P], v_tok[:, c, n * P:(n + 1) * P], ws[:, c, :],
                             start=True, stop=True)
                ins.then_inc(S["mixed"], 1)
            projections_and_squares("ev_out", 1, 1)
            peer_pe(0)
            sum_squares(2)
            projections("od_in", OD_IN, 3)
            projections_and_squares("od_out", 4, 3)
            peer_pe(1)
            sum_squares(4)


N_INPUTS = 2
N_LATE_INPUTS = 3
MOD_A_ORDER = list(range(KC, 2 * KC)) + list(range(KC))
ROOTS_BEFORE = (0, 3, 4, 5, 6)
RESIDUAL = (1, 3)
XR = [0, KC, 2 * KC, 3 * KC, 4 * KC]
HR = [0, 2 * KC, 3 * KC, 5 * KC, 6 * KC]


def kernel(**inputs):
    import concourse.bacc as bacc
    from concourse.bass_utils import run_bass_kernel_spmd

    a = {n: np.asarray(v) for n, v in inputs.items()}

    def tiles(w, order=None):
        t = w.reshape(KC, P, -1, P).transpose(2, 1, 0, 3)
        return t if order is None else t[order]

    ev_order = [i for c in range(AC) for i in (c, AC + c)] + [3 * AC + c for c in range(AC)] \
        + [2 * AC + c for c in range(AC)]
    od_order = [i for c in range(KC) for i in (KC + c, 2 * KC + c, c)]
    parts = []
    for l in range(2):
        if l == 0:
            parts += [tiles(a["ev_w_in"][0], ev_order), tiles(a["ev_w_out"][0])]
        else:
            parts += [tiles(a["od_w_in"][0], od_order), tiles(a["od_w_out"][0])]
        parts.append(tiles(a["pk_wq"][l]))
        parts.append(a["pk_u"][l].reshape(NK, NK, KC, P).transpose(1, 3, 2, 0))
        parts.append(a["pk_v"][l].reshape(NK, NK, D).transpose(1, 0, 2).reshape(NK, P, KC, P))
    stream = np.empty((TILES, P, D), a["x"].dtype)
    at = 0
    for p in parts:
        stream[at:at + len(p)].reshape(len(p), P, KC, P)[:] = p
        at += len(p)
    assert at == TILES
    mod_rows = a["mod_w"].transpose(0, 2, 1).reshape(MOD, P, D)

    def columns(v):
        return v.reshape(-1, P).T

    cols = np.concatenate([
        columns(a["mod_b"]), columns(a["norm1_g"]), columns(a["norm2_g"]),
        a["ev_conv_w"][0].reshape(TAPS, AC, P).transpose(2, 1, 0).reshape(P, AC * TAPS),
        columns(a["ev_conv_b"]), columns(a["ev_cln_g"]), columns(a["ev_cln_b"]), columns(a["ev_gln_g"]),
        columns(a["ev_gln_b"]), a["od_conv_w"][0].reshape(3, KC, P).transpose(2, 1, 0).reshape(P, 3 * KC),
        columns(a["final_g"])], axis=1)
    arrays = {
        "stream": stream,
        "mod_rows": mod_rows,
        "c_in": np.broadcast_to(a["c"], (P, D)),
        "x_in": a["x"][0].T.reshape(KC, P, T).transpose(1, 0, 2),
        "cols_in": cols,
        "sk_in": a["pk_subkeys"].transpose(3, 0, 1, 2),
        "ws_in": a["ev_ws"][0].transpose(2, 0, 1),
        "bs_in": np.broadcast_to(a["ev_bs"][0][None], (P, AC, P)),
    }
    arrays = {n: np.ascontiguousarray(v) for n, v in arrays.items()}
    nc = bacc.Bacc("TRN2", target_bir_lowering=False, num_devices=1)
    args = {n: nc.dram_tensor(n, v.shape, mybir.dt.from_np(v.dtype), kind="ExternalInput").ap()
            for n, v in arrays.items()}
    out = nc.dram_tensor("out", [P, KC, T], F32, kind="ExternalOutput").ap()
    act_dram = nc.dram_tensor("act_dram", [EXPERT_TILES, P, T], F32).ap()
    gate_dram = nc.dram_tensor("gate_dram", [T // HALF, P, NK, HALF], F32).ap()
    build(nc, out=out, act_dram=act_dram, gate_dram=gate_dram, **args)
    r = run_bass_kernel_spmd(nc, [arrays], core_ids=[0])
    got = r.results[0]["out"]
    return np.ascontiguousarray(got.transpose(2, 1, 0).reshape(1, T, D))
```
